# Optimizing a Trainium2 kernel written in Bass

```python
import jax, jax.numpy as jnp
from jax import lax
import numpy as np
import math

D_MODEL = 2048
BATCH = 1
SEQ = 256
DEPTH = 1

MIX_WIDTH = D_MODEL
GROUP_WIDTH = MIX_WIDTH // 4
HEAD_DIM = 128
N_HEADS_PER_MIXER = GROUP_WIDTH // HEAD_DIM
CHUNK = 128
SHORT_CONV = 3
CONFORMER_CONV = 31
POOL_WINDOWS = (2, 4, 8, 16)
POOL_GROUP = GROUP_WIDTH // len(POOL_WINDOWS)
D_FF = ((8 * D_MODEL // 3 + 255) // 256) * 256
PLE_DIM = 256
EPS = 1e-6
A_COLS = 2 * GROUP_WIDTH
B_COLS = 3 * GROUP_WIDTH
C_COLS = 2 * GROUP_WIDTH
D_COLS = GROUP_WIDTH
IN_COLS = A_COLS + B_COLS + C_COLS + D_COLS


def _rms(x, g):
    xf = x.astype(jnp.float32)
    y = xf * lax.rsqrt(jnp.mean(xf * xf, axis=-1, keepdims=True) + EPS)
    return (y * g.astype(jnp.float32)).astype(x.dtype)

def _ln(x, g, b):
    xf = x.astype(jnp.float32)
    mu = jnp.mean(xf, axis=-1, keepdims=True)
    xc = xf - mu
    var = jnp.mean(xc * xc, axis=-1, keepdims=True)
    y = xc * lax.rsqrt(var + EPS) * g.astype(jnp.float32) + b.astype(jnp.float32)
    return y.astype(x.dtype)

def _causal_dwconv(x, w):
    k, c = w.shape
    return lax.conv_general_dilated(
        x, w[:, None, :].astype(x.dtype), window_strides=(1,), padding=[(k - 1, 0)],
        dimension_numbers=("NWC", "WIO", "NWC"), feature_group_count=c)

def _mixer_sgu(z, ln_g, ln_b, w_s, b_s):
    bsz, s, _ = z.shape
    n = s // CHUNK
    z = jax.nn.gelu(z)
    u, v = jnp.split(z, 2, axis=-1)
    v = _ln(v.reshape(bsz, s, N_HEADS_PER_MIXER, HEAD_DIM), ln_g, ln_b)
    v = v.reshape(bsz, n, CHUNK, N_HEADS_PER_MIXER, HEAD_DIM)
    mask = jnp.tril(jnp.ones((CHUNK, CHUNK), dtype=bool))
    wm = jnp.where(mask[None], w_s, jnp.zeros((), w_s.dtype))
    sp = jnp.einsum("hts,bnshd->bnthd", wm, v) + b_s.T[:, :, None]
    out = u.reshape(bsz, n, CHUNK, N_HEADS_PER_MIXER, HEAD_DIM) * sp
    return out.reshape(bsz, s, GROUP_WIDTH)

def _mixer_shortconv(z, conv_w):
    h, bg, cg = jnp.split(z, 3, axis=-1)
    return bg * _causal_dwconv(cg * h, conv_w)

def _mixer_conformer(z, conv_w, conv_b, ln_g, ln_b):
    a, g = jnp.split(z, 2, axis=-1)
    h = a * jax.nn.sigmoid(g)
    h = _causal_dwconv(h, conv_w) + conv_b
    h = _ln(h, ln_g, ln_b)
    return jax.nn.silu(h)

def _mixer_pool(z, pool_w, pool_scale):
    bsz, s, _ = z.shape
    zg = z.reshape(bsz, s, len(POOL_WINDOWS), POOL_GROUP)
    cs = jnp.cumsum(zg.astype(jnp.float32), axis=1)
    pos = jnp.arange(1, s + 1, dtype=jnp.int32)
    pooled = []
    for gi, w in enumerate(POOL_WINDOWS):
        c = cs[:, :, gi]
        lagged = jnp.pad(c, ((0, 0), (w, 0), (0, 0)))[:, :s]
        count = jnp.minimum(pos, w).astype(jnp.float32)
        pooled.append((c - lagged) / count[None, :, None])
    pooled = jnp.stack(pooled, axis=2).astype(z.dtype) - zg
    out = jnp.einsum("bsgc,gcd->bsgd", pooled, pool_w).reshape(bsz, s, GROUP_WIDTH)
    return out * pool_scale

def first_inputs(seed: int = 0) -> dict:
    key = jax.random.key(seed)
    ks = jax.random.split(key, 24)
    f = jnp.float32
    L, D, G, H, hd = DEPTH, D_MODEL, GROUP_WIDTH, N_HEADS_PER_MIXER, HEAD_DIM
    nrm = lambda k, shape, scale: jax.random.normal(k, shape, f) * scale
    gain = lambda k, shape: 1.0 + 0.05 * jax.random.normal(k, shape, f)
    return {
        "x": jax.random.normal(ks[0], (BATCH, SEQ, D), f),
        "p": jax.random.normal(ks[1], (DEPTH, BATCH, SEQ, PLE_DIM), f),
        "norm_mix_g": gain(ks[2], (L, D)),
        "w_in": nrm(ks[3], (L, D, IN_COLS), D ** -0.5),
        "sgu_ln_g": gain(ks[4], (L, H, hd)),
        "sgu_ln_b": nrm(ks[5], (L, H, hd), 0.02),
        "sgu_w": nrm(ks[6], (L, H, CHUNK, CHUNK), CHUNK ** -0.5),
        "sgu_b": gain(ks[7], (L, H, CHUNK)),
        "sc_conv_w": nrm(ks[8], (L, SHORT_CONV, G), SHORT_CONV ** -0.5),
        "cf_conv_w": nrm(ks[9], (L, CONFORMER_CONV, G), CONFORMER_CONV ** -0.5),
        "cf_conv_b": nrm(ks[10], (L, G), 0.02),
        "cf_ln_g": gain(ks[11], (L, G)),
        "cf_ln_b": nrm(ks[12], (L, G), 0.02),
        "pool_w": nrm(ks[13], (L, len(POOL_WINDOWS), POOL_GROUP, POOL_GROUP), POOL_GROUP ** -0.5),
        "pool_scale": 0.5 + 0.1 * jax.random.normal(ks[14], (L, G), f),
        "w_out": nrm(ks[15], (L, MIX_WIDTH, D), MIX_WIDTH ** -0.5),
        "norm_ffn_g": gain(ks[16], (L, D)),
        "w_gate": nrm(ks[17], (L, D, D_FF), D ** -0.5),
        "w_up": nrm(ks[18], (L, D, D_FF), D ** -0.5),
        "w_down": nrm(ks[19], (L, D_FF, D), D_FF ** -0.5),
        "norm_ple_g": gain(ks[20], (L, D)),
        "w_ple_gate": nrm(ks[21], (L, D, D), D ** -0.5),
        "w_ple_proj": nrm(ks[22], (L, PLE_DIM, D), PLE_DIM ** -0.5),
        "final_norm_g": gain(ks[23], (D,)),
    }

def first_block(x, p, norm_mix_g, w_in, sgu_ln_g, sgu_ln_b, sgu_w, sgu_b, sc_conv_w,
              cf_conv_w, cf_conv_b, cf_ln_g, cf_ln_b, pool_w, pool_scale, w_out,
              norm_ffn_g, w_gate, w_up, w_down, norm_ple_g, w_ple_gate, w_ple_proj,
              final_norm_g):
    h = x
    split_at = [A_COLS, A_COLS + B_COLS, A_COLS + B_COLS + C_COLS]
    for i in range(DEPTH):
        y = _rms(h, norm_mix_g[i])
        z = y @ w_in[i]
        za, zb, zc, zd = jnp.split(z, split_at, axis=-1)
        oa = _mixer_sgu(za, sgu_ln_g[i], sgu_ln_b[i], sgu_w[i], sgu_b[i])
        ob = _mixer_shortconv(zb, sc_conv_w[i])
        oc = _mixer_conformer(zc, cf_conv_w[i], cf_conv_b[i], cf_ln_g[i], cf_ln_b[i])
        od = _mixer_pool(zd, pool_w[i], pool_scale[i])
        h = h + jnp.concatenate([oa, ob, oc, od], axis=-1) @ w_out[i]
        y = _rms(h, norm_ffn_g[i])
        h = h + (jax.nn.silu(y @ w_gate[i]) * (y @ w_up[i])) @ w_down[i]
        y = _rms(h, norm_ple_g[i])
        h = h + jax.nn.sigmoid(y @ w_ple_gate[i]) * (p[i] @ w_ple_proj[i])
    return _rms(h, final_norm_g)


N_MIXERS = 4
N_SWA = (DEPTH + 3) // N_MIXERS
N_RWKV = (DEPTH + 2) // N_MIXERS
N_MLSTM = (DEPTH + 1) // N_MIXERS
N_FOX = DEPTH // N_MIXERS

SWA_HEAD_DIM = 64
SWA_HEADS = D_MODEL // SWA_HEAD_DIM
SWA_KV_HEADS = SWA_HEADS // 8
SWA_GROUP = SWA_HEADS // SWA_KV_HEADS
SWA_WIDTH = SWA_HEADS * SWA_HEAD_DIM
SWA_KV_WIDTH = SWA_KV_HEADS * SWA_HEAD_DIM
SWA_IN = 2 * SWA_WIDTH + 2 * SWA_KV_WIDTH
SWA_WINDOW = 128
SWA_BLOCK = 128
REL_BUCKETS = 32
REL_MAX_DIST = 128
RWKV_HEAD_DIM = 64
RWKV_HEADS = D_MODEL // RWKV_HEAD_DIM
RWKV_DECAY_LORA = 96
RWKV_AAA_LORA = 96
RWKV_N_MIX = 6
MLSTM_HEADS = 8
MLSTM_V_DIM = D_MODEL // MLSTM_HEADS
MLSTM_QK_DIM = MLSTM_V_DIM // 2
MLSTM_QK_WIDTH = MLSTM_HEADS * MLSTM_QK_DIM
MLSTM_V_WIDTH = MLSTM_HEADS * MLSTM_V_DIM
MLSTM_IN = 2 * MLSTM_QK_WIDTH + 3 * MLSTM_V_WIDTH + 2 * MLSTM_HEADS
MLSTM_CHUNK = 128
FOX_HEAD_DIM = 64
FOX_HEADS = D_MODEL // FOX_HEAD_DIM
FOX_WIDTH = FOX_HEADS * FOX_HEAD_DIM
FOX_IN = 4 * FOX_WIDTH + FOX_HEADS
FOX_BLOCK = 128

RMS_EPS = 1e-6
GN_EPS = 64e-5


def rms_norm(x, g):
    xf = x.astype(jnp.float32)
    y = xf * lax.rsqrt(jnp.mean(xf * xf, axis=-1, keepdims=True) + RMS_EPS)
    return (y * g.astype(jnp.float32)).astype(x.dtype)

def t5_bucket(dist):
    max_exact = REL_BUCKETS // 2
    d_f = jnp.maximum(dist, 1).astype(jnp.float32)
    large = max_exact + (jnp.log(d_f / max_exact) / math.log(REL_MAX_DIST / max_exact)
                         * (REL_BUCKETS - max_exact)).astype(jnp.int32)
    large = jnp.minimum(large, REL_BUCKETS - 1)
    return jnp.where(dist < max_exact, dist, large)

def swa_sink_mixer(h, w_in, q_gain, k_gain, sinks, rel_table, w_out):
    bsz, seq, _ = h.shape
    L = SWA_BLOCK
    nb = seq // L
    q, k, v, gate = jnp.split(h @ w_in, [SWA_WIDTH, SWA_WIDTH + SWA_KV_WIDTH,
                                         SWA_WIDTH + 2 * SWA_KV_WIDTH], axis=-1)
    q = rms_norm(q.reshape(bsz, seq, SWA_KV_HEADS, SWA_GROUP, SWA_HEAD_DIM), q_gain)
    k = rms_norm(k.reshape(bsz, seq, SWA_KV_HEADS, SWA_HEAD_DIM), k_gain)
    v = v.reshape(bsz, seq, SWA_KV_HEADS, SWA_HEAD_DIM)
    pad = ((0, 0), (L, 0), (0, 0), (0, 0))
    k_pad = jnp.pad(k, pad)
    v_pad = jnp.pad(v, pad)
    qi = jnp.arange(L)[:, None]
    kj = jnp.arange(2 * L)[None, :]
    dist = qi + L - kj
    in_band = (dist >= 0) & (dist < SWA_WINDOW)
    bias = rel_table.astype(jnp.float32)[t5_bucket(jnp.maximum(dist, 0))]
    bias = bias.transpose(2, 0, 1).reshape(SWA_KV_HEADS, SWA_GROUP, L, 2 * L)
    sink = sinks.astype(jnp.float32).reshape(SWA_KV_HEADS, SWA_GROUP, 1, 1)
    scale = SWA_HEAD_DIM ** -0.5
    q_blocks = q.reshape(bsz, nb, L, SWA_KV_HEADS, SWA_GROUP, SWA_HEAD_DIM).transpose(1, 0, 2, 3, 4, 5)

    def one_block(args):
        j, qj = args
        start = j * L
        kb = lax.dynamic_slice_in_dim(k_pad, start, 2 * L, axis=1)
        vb = lax.dynamic_slice_in_dim(v_pad, start, 2 * L, axis=1)
        s = jnp.einsum('bqhgd,bkhd->bhgqk', qj, kb).astype(jnp.float32) * scale + bias
        valid = in_band & (start - L + kj >= 0)
        s = jnp.where(valid, s, -jnp.inf)
        m = jnp.maximum(jnp.max(s, axis=-1, keepdims=True), sink)
        p = jnp.exp(s - m)
        p = p / (jnp.sum(p, axis=-1, keepdims=True) + jnp.exp(sink - m))
        return jnp.einsum('bhgqk,bkhd->bqhgd', p.astype(vb.dtype), vb)

    o = lax.map(one_block, (jnp.arange(nb), q_blocks))
    o = o.transpose(1, 0, 2, 3, 4, 5).reshape(bsz, seq, SWA_WIDTH)
    return (o * jax.nn.silu(gate)) @ w_out

def rwkv7_mixer(h, mix, w_in, w0, w_lora1, w_lora2, a0, a_lora1, a_lora2,
                k_k, k_a, r_k, gn_w, gn_b, w_out):
    bsz, seq, d = h.shape
    H, N = RWKV_HEADS, RWKV_HEAD_DIM
    f32 = jnp.float32
    xx = jnp.pad(h, ((0, 0), (1, 0), (0, 0)))[:, :-1] - h
    xm = h[None] + xx[None] * mix[:, None, None, :]
    r, k, v, g = jnp.einsum('cbsd,cde->cbse', xm[:4], w_in)
    w_pre = (w0 + jnp.tanh(xm[4] @ w_lora1) @ w_lora2).astype(f32)
    log_w = -jnp.exp(-jax.nn.softplus(-w_pre) - 0.5)
    a = jax.nn.sigmoid((a0 + (xm[5] @ a_lora1) @ a_lora2).astype(f32))

    def heads(t):
        return t.astype(f32).reshape(bsz, seq, H, N)

    r, k, v, a, log_w = heads(r), heads(k), heads(v), heads(a), heads(log_w)
    kk = k * k_k.astype(f32).reshape(H, N)
    kk = kk / jnp.maximum(jnp.sqrt(jnp.sum(kk * kk, axis=-1, keepdims=True)), 1e-12)
    k = k * (1.0 + (a - 1.0) * k_a.astype(f32).reshape(H, N))

    def step(state, inp):
        r_t, w_t, k_t, v_t, kk_t, a_t = inp
        sa = jnp.einsum('bhvk,bhk->bhv', state, -kk_t)
        state = (state * w_t[:, :, None, :]
                 + sa[..., None] * (kk_t * a_t)[:, :, None, :]
                 + v_t[..., None] * k_t[:, :, None, :])
        return state, jnp.einsum('bhvk,bhk->bhv', state, r_t)

    def tm(t):
        return t.transpose(1, 0, 2, 3)

    state0 = jnp.zeros((bsz, H, N, N), f32)
    _, y = lax.scan(step, state0, (tm(r), tm(jnp.exp(log_w)), tm(k), tm(v), tm(kk), tm(a)))
    y = tm(y)
    mu = jnp.mean(y, axis=-1, keepdims=True)
    var = jnp.mean(jnp.square(y - mu), axis=-1, keepdims=True)
    y = ((y - mu) * lax.rsqrt(var + GN_EPS)).reshape(bsz, seq, d) * gn_w + gn_b
    bonus = jnp.sum(r * k * r_k.astype(f32), axis=-1, keepdims=True) * v
    y = y + bonus.reshape(bsz, seq, d)
    return (y.astype(h.dtype) * jax.nn.silu(g)) @ w_out

def mlstm_mixer(h, w_in, b_i, b_f, h_gain, w_out):
    bsz, seq, _ = h.shape
    H, dk, dv, L = MLSTM_HEADS, MLSTM_QK_DIM, MLSTM_V_DIM, MLSTM_CHUNK
    nc = seq // L
    f32 = jnp.float32
    s1 = MLSTM_QK_WIDTH
    s2 = s1 + MLSTM_QK_WIDTH
    s3 = s2 + MLSTM_V_WIDTH
    s4 = s3 + MLSTM_V_WIDTH
    s5 = s4 + MLSTM_V_WIDTH
    s6 = s5 + H
    q, k, v, o_pre, gate, i_pre, f_pre = jnp.split(h @ w_in, [s1, s2, s3, s4, s5, s6], axis=-1)
    q = q.astype(f32).reshape(bsz, seq, H, dk) * dk ** -0.5
    k = k.astype(f32).reshape(bsz, seq, H, dk)
    v = v.astype(f32).reshape(bsz, seq, H, dv)
    i_log = (i_pre + b_i).astype(f32)
    f_log = jax.nn.log_sigmoid((f_pre + b_f).astype(f32))

    def chunks(t):
        t = t.reshape((bsz, nc, L) + t.shape[2:])
        return jnp.moveaxis(t, (1, 3), (0, 2))

    tri = jnp.tril(jnp.ones((L, L), dtype=bool))

    def chunk_step(carry, inp):
        C, n, m = carry
        qc, kc, vc, ic, fc = inp
        b = jnp.cumsum(fc, axis=-1)
        g = b[..., -1]
        dmat = jnp.where(tri, b[..., :, None] - b[..., None, :] + ic[..., None, :], -jnp.inf)
        inter = b + m[..., None]
        m_t = jnp.maximum(inter, jnp.max(dmat, axis=-1))
        w_intra = jnp.exp(dmat - m_t[..., None])
        w_inter = jnp.exp(inter - m_t)
        sw = jnp.einsum('bhtd,bhsd->bhts', qc, kc) * w_intra
        num = (w_inter[..., None] * jnp.einsum('bhvk,bhtk->bhtv', C, qc)
               + jnp.einsum('bhts,bhsv->bhtv', sw, vc))
        den = w_inter * jnp.einsum('bhk,bhtk->bht', n, qc) + jnp.sum(sw, axis=-1)
        h_t = num / jnp.maximum(jnp.abs(den), jnp.exp(-m_t))[..., None]
        decay_s = g[..., None] - b + ic
        m_new = jnp.maximum(g + m, jnp.max(decay_s, axis=-1))
        ws = jnp.exp(decay_s - m_new[..., None])
        carry_scale = jnp.exp(g + m - m_new)
        C = carry_scale[..., None, None] * C + jnp.einsum('bhs,bhsv,bhsk->bhvk', ws, vc, kc)
        n = carry_scale[..., None] * n + jnp.einsum('bhs,bhsk->bhk', ws, kc)
        return (C, n, m_new), h_t

    carry0 = (jnp.zeros((bsz, H, dv, dk), f32), jnp.zeros((bsz, H, dk), f32), jnp.zeros((bsz, H), f32))
    _, hs = lax.scan(chunk_step, carry0, (chunks(q), chunks(k), chunks(v), chunks(i_log), chunks(f_log)))
    hs = jnp.moveaxis(hs, (0, 2), (1, 3)).reshape(bsz, seq, H, dv)
    hs = rms_norm(hs, h_gain).reshape(bsz, seq, MLSTM_V_WIDTH).astype(h.dtype)
    return (hs * jax.nn.sigmoid(o_pre) * jax.nn.silu(gate)) @ w_out

def fox_mixer(h, w_in, b_f, q_gain, k_gain, w_out):
    bsz, seq, _ = h.shape
    H, dh, L = FOX_HEADS, FOX_HEAD_DIM, FOX_BLOCK
    nb = seq // L
    W = FOX_WIDTH
    q, k, v, gate, f_pre = jnp.split(h @ w_in, [W, 2 * W, 3 * W, 4 * W], axis=-1)
    q = rms_norm(q.reshape(bsz, seq, H, dh), q_gain)
    k = rms_norm(k.reshape(bsz, seq, H, dh), k_gain)
    v = v.reshape(bsz, seq, H, dh)
    log_f = jax.nn.log_sigmoid((f_pre + b_f).astype(jnp.float32))
    F = jnp.cumsum(log_f, axis=1).transpose(0, 2, 1)
    q_blocks = q.reshape(bsz, nb, L, H, dh).transpose(1, 0, 2, 3, 4)
    F_blocks = F.reshape(bsz, H, nb, L).transpose(2, 0, 1, 3)
    key_pos = jnp.arange(seq)
    scale = dh ** -0.5

    def one_block(args):
        j, qj, Fj = args
        s = (jnp.einsum('bqhd,bkhd->bhqk', qj, k).astype(jnp.float32) * scale
             + (Fj[..., :, None] - F[:, :, None, :]))
        q_pos = j * L + jnp.arange(L)
        s = jnp.where(key_pos[None, :] <= q_pos[:, None], s, -jnp.inf)
        p = jax.nn.softmax(s, axis=-1)
        return jnp.einsum('bhqk,bkhd->bqhd', p.astype(v.dtype), v)

    o = lax.map(one_block, (jnp.arange(nb), q_blocks, F_blocks))
    o = o.transpose(1, 0, 2, 3, 4).reshape(bsz, seq, W)
    return (o * jax.nn.silu(gate)) @ w_out

def second_inputs(seed: int = 0) -> dict:
    key = jax.random.key(seed)
    keys = jax.random.split(key, 48)
    counter = [0]

    def next_key():
        kk = keys[counter[0]]
        counter[0] += 1
        return kk

    def nrm(shape, scale):
        return jax.random.normal(next_key(), shape, jnp.float32) * scale

    def gain(shape):
        return 1.0 + nrm(shape, 0.05)

    D = D_MODEL
    return {
        "x": nrm((BATCH, SEQ, D), 1.0),
        "rel_bias": nrm((REL_BUCKETS, SWA_HEADS), 0.2),
        "swa_norm": gain((N_SWA, D)),
        "swa_w_in": nrm((N_SWA, D, SWA_IN), D ** -0.5),
        "swa_q_gain": gain((N_SWA, SWA_HEAD_DIM)),
        "swa_k_gain": gain((N_SWA, SWA_HEAD_DIM)),
        "swa_sinks": nrm((N_SWA, SWA_HEADS), 0.5),
        "swa_w_out": nrm((N_SWA, SWA_WIDTH, D), SWA_WIDTH ** -0.5),
        "rwkv_norm": gain((N_RWKV, D)),
        "rwkv_mix": jax.random.uniform(next_key(), (N_RWKV, RWKV_N_MIX, D), jnp.float32),
        "rwkv_w_in": nrm((N_RWKV, 4, D, D), D ** -0.5),
        "rwkv_w0": -2.0 + nrm((N_RWKV, D), 1.0),
        "rwkv_w_lora1": nrm((N_RWKV, D, RWKV_DECAY_LORA), D ** -0.5),
        "rwkv_w_lora2": nrm((N_RWKV, RWKV_DECAY_LORA, D), 0.5 * RWKV_DECAY_LORA ** -0.5),
        "rwkv_a0": nrm((N_RWKV, D), 0.1),
        "rwkv_a_lora1": nrm((N_RWKV, D, RWKV_AAA_LORA), D ** -0.5),
        "rwkv_a_lora2": nrm((N_RWKV, RWKV_AAA_LORA, D), 0.5 * RWKV_AAA_LORA ** -0.5),
        "rwkv_k_k": 0.85 + nrm((N_RWKV, D), 0.05),
        "rwkv_k_a": 1.0 + nrm((N_RWKV, D), 0.05),
        "rwkv_r_k": nrm((N_RWKV, RWKV_HEADS, RWKV_HEAD_DIM), 0.1),
        "rwkv_gn_w": gain((N_RWKV, D)),
        "rwkv_gn_b": nrm((N_RWKV, D), 0.02),
        "rwkv_w_out": nrm((N_RWKV, D, D), D ** -0.5),
        "mlstm_norm": gain((N_MLSTM, D)),
        "mlstm_w_in": nrm((N_MLSTM, D, MLSTM_IN), D ** -0.5),
        "mlstm_b_i": nrm((N_MLSTM, MLSTM_HEADS), 0.1),
        "mlstm_b_f": 3.0 + nrm((N_MLSTM, MLSTM_HEADS), 0.5),
        "mlstm_h_gain": gain((N_MLSTM, MLSTM_HEADS, MLSTM_V_DIM)),
        "mlstm_w_out": nrm((N_MLSTM, MLSTM_V_WIDTH, D), MLSTM_V_WIDTH ** -0.5),
        "fox_norm": gain((N_FOX, D)),
        "fox_w_in": nrm((N_FOX, D, FOX_IN), D ** -0.5),
        "fox_b_f": 3.0 + nrm((N_FOX, FOX_HEADS), 0.5),
        "fox_q_gain": gain((N_FOX, FOX_HEAD_DIM)),
        "fox_k_gain": gain((N_FOX, FOX_HEAD_DIM)),
        "fox_w_out": nrm((N_FOX, FOX_WIDTH, D), FOX_WIDTH ** -0.5),
    }

def second_block(x, rel_bias, swa_norm, swa_w_in, swa_q_gain, swa_k_gain, swa_sinks, swa_w_out,
              rwkv_norm, rwkv_mix, rwkv_w_in, rwkv_w0, rwkv_w_lora1, rwkv_w_lora2, rwkv_a0,
              rwkv_a_lora1, rwkv_a_lora2, rwkv_k_k, rwkv_k_a, rwkv_r_k, rwkv_gn_w, rwkv_gn_b,
              rwkv_w_out, mlstm_norm, mlstm_w_in, mlstm_b_i, mlstm_b_f, mlstm_h_gain, mlstm_w_out,
              fox_norm, fox_w_in, fox_b_f, fox_q_gain, fox_k_gain, fox_w_out):
    for layer in range(DEPTH):
        kind, idx = layer % N_MIXERS, layer // N_MIXERS
        if kind == 0:
            x = x + swa_sink_mixer(rms_norm(x, swa_norm[idx]), swa_w_in[idx], swa_q_gain[idx],
                                   swa_k_gain[idx], swa_sinks[idx], rel_bias, swa_w_out[idx])
        elif kind == 1:
            x = x + rwkv7_mixer(rms_norm(x, rwkv_norm[idx]), rwkv_mix[idx], rwkv_w_in[idx],
                                rwkv_w0[idx], rwkv_w_lora1[idx], rwkv_w_lora2[idx], rwkv_a0[idx],
                                rwkv_a_lora1[idx], rwkv_a_lora2[idx], rwkv_k_k[idx], rwkv_k_a[idx],
                                rwkv_r_k[idx], rwkv_gn_w[idx], rwkv_gn_b[idx], rwkv_w_out[idx])
        elif kind == 2:
            x = x + mlstm_mixer(rms_norm(x, mlstm_norm[idx]), mlstm_w_in[idx], mlstm_b_i[idx],
                                mlstm_b_f[idx], mlstm_h_gain[idx], mlstm_w_out[idx])
        else:
            x = x + fox_mixer(rms_norm(x, fox_norm[idx]), fox_w_in[idx], fox_b_f[idx],
                              fox_q_gain[idx], fox_k_gain[idx], fox_w_out[idx])
    return x


def setup_inputs(seed=0):
    out = dict(first_inputs(seed))
    for name, value in second_inputs(seed + 1).items():
        if name != "x":
            out[name + "_2"] = value
    return out


def reference(
    x, p, norm_mix_g, w_in, sgu_ln_g, sgu_ln_b, sgu_w, sgu_b, sc_conv_w, cf_conv_w, cf_conv_b,
    cf_ln_g, cf_ln_b, pool_w, pool_scale, w_out, norm_ffn_g, w_gate, w_up, w_down, norm_ple_g,
    w_ple_gate, w_ple_proj, final_norm_g, rel_bias_2, swa_norm_2, swa_w_in_2, swa_q_gain_2,
    swa_k_gain_2, swa_sinks_2, swa_w_out_2, rwkv_norm_2, rwkv_mix_2, rwkv_w_in_2, rwkv_w0_2,
    rwkv_w_lora1_2, rwkv_w_lora2_2, rwkv_a0_2, rwkv_a_lora1_2, rwkv_a_lora2_2, rwkv_k_k_2,
    rwkv_k_a_2, rwkv_r_k_2, rwkv_gn_w_2, rwkv_gn_b_2, rwkv_w_out_2, mlstm_norm_2, mlstm_w_in_2,
    mlstm_b_i_2, mlstm_b_f_2, mlstm_h_gain_2, mlstm_w_out_2, fox_norm_2, fox_w_in_2, fox_b_f_2,
    fox_q_gain_2, fox_k_gain_2, fox_w_out_2,
):
    x = first_block(
        x, p, norm_mix_g, w_in, sgu_ln_g, sgu_ln_b, sgu_w, sgu_b, sc_conv_w, cf_conv_w,
        cf_conv_b, cf_ln_g, cf_ln_b, pool_w, pool_scale, w_out, norm_ffn_g, w_gate, w_up,
        w_down, norm_ple_g, w_ple_gate, w_ple_proj, final_norm_g,
    )
    return second_block(
        x, rel_bias_2, swa_norm_2, swa_w_in_2, swa_q_gain_2, swa_k_gain_2, swa_sinks_2,
        swa_w_out_2, rwkv_norm_2, rwkv_mix_2, rwkv_w_in_2, rwkv_w0_2, rwkv_w_lora1_2,
        rwkv_w_lora2_2, rwkv_a0_2, rwkv_a_lora1_2, rwkv_a_lora2_2, rwkv_k_k_2, rwkv_k_a_2,
        rwkv_r_k_2, rwkv_gn_w_2, rwkv_gn_b_2, rwkv_w_out_2, mlstm_norm_2, mlstm_w_in_2,
        mlstm_b_i_2, mlstm_b_f_2, mlstm_h_gain_2, mlstm_w_out_2, fox_norm_2, fox_w_in_2,
        fox_b_f_2, fox_q_gain_2, fox_k_gain_2, fox_w_out_2,
    )


_drawn_inputs = setup_inputs


def setup_inputs(seed=0):
    import zlib

    import numpy as np

    out = dict(_drawn_inputs(seed))
    spreads = {}
    factors = {'sgu_ln_g': 5.931,
     'sgu_ln_b': 8.0,
     'sgu_b': 4.144,
     'cf_conv_b': 4.358,
     'cf_ln_g': 3.477,
     'cf_ln_b': 8.0,
     'norm_ple_g': 7.846,
     'rel_bias_2': 2.821,
     'swa_norm_2': 4.48,
     'swa_q_gain_2': 8.0,
     'swa_k_gain_2': 8.0,
     'swa_sinks_2': 32.509}
    for name, (base, spread) in spreads.items():
        noise = np.random.default_rng([zlib.crc32(name.encode()), seed]).standard_normal(out[name].shape)
        drawn = base * np.exp(spread * noise) if base else spread * noise
        out[name] = __import__('jax').numpy.asarray(drawn.astype(out[name].dtype))
    for name, factor in factors.items():
        out[name] = (out[name] * factor).astype(out[name].dtype)
    return out
```

```python
import numpy as np
from contextlib import ExitStack

import concourse.bass as bass
import concourse.mybir as mybir

F32 = mybir.dt.float32
F32R = mybir.dt.float32r
ALU = mybir.AluOpType
ACT = mybir.ActivationFunctionType
AX = mybir.AxisListType.X

P = 128
D = 2048
S = 256
T = S // P
CW = 512
NG = D // CW
KT = D // P
CK = 2
EPS = 1e-6
RAW = 8
SPL = 4
TAPS = 31
WINDOWS = (2, 4, 8, 16)
HD = 64
HG = 8
MASKED = -1e30

IN_ORDER = (6, 5, 2, 4, 3, 7, 1, 0)
U_G, U_A, U_H, U_CG, U_BG, U_D, U_V, U_U = range(8)
OUT_ROWS = (4, 6, 12, 14, 0, 2, 8, 10)
SWA_ORDER = (4, 0, 1, 2, 3, 5, 6, 7, 8)

UNITS = [(8, e) for e in "adadaaaa"]
UNITS += [(1, "a")] * 4
UNITS += [(8, "d")] * 4
FFN_UNIT = len(UNITS)
for _round in range(3):
    _pairs = 4 if _round < 2 else 3
    UNITS += [(8, "a"), (8, "d")] * _pairs
    UNITS += [(2 * _pairs, "d")] * 4
PLE_UNIT = len(UNITS)
UNITS += [(8, "a")] * 4
SWA_UNIT = len(UNITS)
UNITS += [(8, "a")] * 9
SO_UNIT = len(UNITS)
UNITS += [(8, "d")] * 4
START = [sum(n for n, _ in UNITS[:u]) for u in range(len(UNITS) + 1)]
PROJ_UNIT, OUT_UNIT = 8, 12

HALVES = "d" + "xx" * 4 + "d" + "dx" + "aa" + "aa" + "dd" + "aa" + "xx" + "dd" + "aa" + "xx"
H_MIX, H_X, H_VEC, H_INIT, H_HC, H_SC, H_BG, H_PZ, H_PO, H_CB, H_CN, H_OA = 0, 1, 9, 10, 12, 14, 16, 18, 20, 22, 24, 26
H_FFN = len(HALVES)
HALVES += "xx" * 4
H_HID = len(HALVES)
HALVES += "xx" * 11
H_PLE = len(HALVES)
HALVES += "xx" * 4
H_SWA = len(HALVES)
HALVES += "xx" * 4
H_K = len(HALVES)
HALVES += "aa"
H_Q, H_PT, H_PV, H_OG = {}, {}, {}, {}
for _g in range(5):
    if _g == 0:
        H_Q[0] = len(HALVES)
        HALVES += "aa"
        continue
    q = _g - 1
    H_PT[q, 0] = len(HALVES); HALVES += "aa"
    H_PV[q, 0] = len(HALVES); HALVES += "d"
    H_PT[q, 1] = len(HALVES); HALVES += "aa"
    if _g < 4:
        H_Q[_g] = len(HALVES); HALVES += "aa"
    else:
        H_OG[0] = len(HALVES); HALVES += "xx"
    H_PV[q, 1] = len(HALVES); HALVES += "d"
    H_PT[q, 2] = len(HALVES); HALVES += "aa"
    H_PV[q, 2] = len(HALVES); HALVES += "d"
for _g in range(1, 4):
    H_OG[_g] = len(HALVES); HALVES += "xx"
ROUNDS = ((0, 0, 8, 1), (1, 0, 4, 2), (1, 4, 4, 2))


BUSY = (35, 40, 47, 56, 57, 60, 61, 62, 63)


class Lap:

    def __init__(self, oct=0, a=0, d=0, h=0):
        self.oct, self.a, self.d, self.h = oct, a, d, h

    @classmethod
    def at(cls, r, j=0):
        return cls(12 * r + 2 * j, 4 * r + j, 8 * r + j, 8 * r + 2 * j)


ONCE = Lap()


def bucket_rows():
    n = np.arange(3 * P)
    dist = n - (P - 1)
    valid = (dist >= 0) & (dist < P)
    dd = np.where(valid, dist, 0)
    exact = 16
    large = exact + (np.log(np.maximum(dd, 1).astype(np.float32) / exact) / np.log(P / exact)
                     * (32 - exact)).astype(np.int32)
    bucket = np.where(dd < exact, dd, np.minimum(large, 31))
    rows = np.zeros((33, 3 * P), np.float32)
    rows[bucket[valid], n[valid]] = 1.0
    rows[32, ~valid] = MASKED
    return rows


def pool_counts():
    return np.array([[min(t + 1, w) for w in WINDOWS for t in range(16)]], np.float32)


def build(nc, x, p, norm_mix_g, w_in, sgu_ln_g, sgu_ln_b, sgu_w, sgu_b, sc_conv_w, cf_conv_w,
          cf_conv_b, cf_ln_g, cf_ln_b, pool_w, pool_scale, w_out, norm_ffn_g, w_gate, w_up, w_down,
          norm_ple_g, w_ple_gate, w_ple_proj, final_norm_g, rel_bias, swa_norm, swa_w_in,
          swa_q_gain, swa_k_gain, swa_sinks, swa_w_out, buckets, counts, out, bias_rows):
    def rows(w):
        return w.rearrange("l (k p) n -> p (l k) n", p=P)

    win_v, wout_v, wg_v, wu_v, wd_v = map(rows, (w_in, w_out, w_gate, w_up, w_down))
    wpg_v, wpp_v, swi_v, swo_v = map(rows, (w_ple_gate, w_ple_proj, swa_w_in, swa_w_out))
    x_v = x.rearrange("b (t p) n -> p (b t) n", p=P)
    out_v = out.rearrange("b (t p) n -> p (b t) n", p=P)

    with ExitStack() as ctx:
        def sb(name, shape, dt=F32):
            return ctx.enter_context(nc.sbuf_tensor(name, shape, dt))

        def bank(name):
            return ctx.enter_context(nc.psum_tensor(name, [P, 512], F32))

        def sem(name):
            return ctx.enter_context(nc.semaphore(name))

        w_raw = sb("w_raw", [P, RAW, CK, CW])
        w_hi = sb("w_hi", [P, SPL, CK, CW], F32R)
        w_lo = sb("w_lo", [P, SPL, CK, CW], F32R)
        yh, yl = sb("yh", [P, KT, S], F32R), sb("yl", [P, KT, S], F32R)
        hh, hl = sb("hh", [P, KT, S], F32R), sb("hl", [P, KT, S], F32R)
        resid = sb("resid", [P, T, D])
        wide = sb("wide", [P, T, D])
        big = sb("big", [P, D])
        tile = [sb(f"tile{i}", [P, 1024]) for i in range(8)]

        def tok(i):
            return tile[i][:].rearrange("p (t n) -> p t n", t=T)

        def feat(i):
            return tile[i][:].rearrange("p (k n) -> p k n", k=4)

        conv_term = wide[:, 0, 3 * CW:4 * CW].rearrange("p (i n) -> p i n", i=2)

        ident = sb("ident", [P, P])
        flip = sb("flip", [P, P])
        vec = sb("vec", [P, 114])
        cw = sb("cw", [P, TAPS * 4])
        gfs = sb("gfs", [P, KT])
        gqk = sb("gqk", [P, 1])
        sinks = sb("sinks", [P, 32])
        rcount = sb("rcount", [P, 4, 16])
        first16 = sb("first16", [P, 4, 16])
        minus_half = sb("minus_half", [P, 16])
        ssq = sb("ssq", [P, 4, T, NG])
        ssq_x1 = sb("ssq_x1", [P, T])
        ms = sb("ms", [P, 12, 16])
        eps_ms = sb("eps_ms", [P, 12, 16])
        rs = sb("rs", [P, 12, 16])
        rr = sb("rr", [P, T])
        st = sb("st", [P, 8, 6])
        mv = sb("mv", [P, 8, 2])
        cst = sb("cst", [P, T, 6])
        cmv = sb("cmv", [P, T, 2])
        smx = sb("smx", [P, 12, 8])
        negm = sb("negm", [P, 12, 8])
        ssink = sb("ssink", [P, 12, 8])
        ssum = sb("ssum", [P, 12, 8])
        rden = sb("rden", [P, 12, 8])

        V_MIX, V_FFN, V_PLE, V_FIN, V_SWA = 0, 16, 32, 48, 64
        V_CB, V_LG, V_LB, V_SC, V_PS, V_SB, V_Q, V_K = 80, 84, 88, 92, 104, 108, 112, 113
        R_X, R_SGU, R_CONF, R_FFN, R_PLE, R_FIN, R_SWA, R_K, R_Q = range(9)

        acc = [[bank(f"acc{i}{t}") for t in range(T)] for i in range(2)]
        tp = [bank(f"tp{i}") for i in range(2)]
        sp = [bank(f"sp{i}") for i in range(2)]

        x_in = [sem(f"x_in{j}") for j in range(NG)]
        mix_in = sem("mix_in")
        params_in = sem("params_in")
        late_in = sem("late_in")
        bias_in = sem("bias_in")
        bias_out = sem("bias_out")
        raw_in = [sem(f"raw_in{i}") for i in range(RAW)]
        hi_ready = sem("hi_ready")
        lo_ready = sem("lo_ready")
        used = sem("used")
        left = {"a": sem("left_act"), "d": sem("left_dve")}
        tp_ready = sem("tp_ready")
        tp_left = {"a": sem("tp_left_act"), "d": sem("tp_left_dve")}
        feat_hi = sem("feat_hi")
        consts = sem("consts")
        masked = sem("masked")
        prod = sem("prod")
        squares = sem("squares")
        want = sem("want")
        eps_done = sem("eps_done")
        got = sem("got")
        vstep = sem("vstep")
        conv = sem("conv")
        conv_terms = sem("conv_terms")
        conv_pool = sem("conv_pool")
        mix_hi = sem("mix_hi")
        mix_ready = sem("mix_ready")
        bias_psum = sem("bias_psum")
        bias_sb = sem("bias_sb")
        sgu_ready = sem("sgu_ready")
        sgu_sum = sem("sgu_sum")
        oa_ready = sem("oa_ready")
        pooled = sem("pooled")
        x1_ready = sem("x1_ready")
        kv_flipped = sem("kv_flipped")
        kv_ready = sem("kv_ready")
        kd_ready = sem("kd_ready")
        q_squares = sem("q_squares")
        scores = sem("scores")
        scored = sem("scored")
        smax = sem("smax")
        expd = sem("expd")
        og_ready = sem("og_ready")
        last_sums = sem("last_sums")
        stored = sem("stored")

        def wait_left(eng, u, lap=ONCE):
            e = UNITS[u][1]
            n = sum(1 for _, o in UNITS[:u + 1] if o == e)
            eng.wait_ge(left[e], n + (lap.a if e == "a" else lap.d))

        def wait_unit(eng, u, lap=ONCE):
            eng.wait_ge(used, START[u + 1] + 8 * lap.oct)

        def taker(h):
            return "a" if HALVES[h] == "a" else "d"

        def wait_half_left(eng, h, lap=ONCE):
            n = sum(1 for i in range(h + 1) if taker(i) == taker(h))
            eng.wait_ge(tp_left[taker(h)], n + (lap.h if taker(h) == "d" else 0))

        def wait_half(eng, h, lap=ONCE):
            eng.wait_ge(tp_ready, h + 1 + lap.h)

        def hi_count(h):
            return sum(1 for i in range(h + 1) if HALVES[i] == "x")

        def bank_of(h):
            return (sp if h in (H_X + 2, H_X + 3, H_X + 6, H_X + 7) else tp)[h % 2]

        def before(h):
            if h in (H_MIX, H_X, H_X + 2, H_X + 3):
                return None
            return h - 4 if H_X + 4 <= h <= H_X + 9 else h - 2

        def half_tile(h):
            return bank_of(h)[:].rearrange("p (k n) -> p k n", k=2)

        vec_rows = ((V_FFN, norm_ffn_g), (V_PLE, norm_ple_g), (V_SWA, swa_norm),
                    (V_CB, cf_conv_b), (V_LG, cf_ln_g), (V_LB, cf_ln_b), (V_PS, pool_scale))
        small_loads = [(tile[0][v:v + g.shape[1] // P, 0:P], g.rearrange("l (k p) -> (l k) p", p=P)) for v, g in vec_rows]
        small_loads += [
            (tile[0][V_FIN:V_FIN + KT, 0:P], final_norm_g.rearrange("(k p) -> k p", p=P)),
            (tile[0][V_SC:V_SC + 12, 0:P], sc_conv_w.rearrange("l k (c p) -> (l k c) p", p=P)),
            (tile[0][V_SB:V_SB + 4, 0:P], sgu_b.rearrange("l h t -> (l h) t")),
            (tile[0][V_Q:V_Q + 1, 0:HD], swa_q_gain), (tile[0][V_Q:V_Q + 1, HD:P], swa_q_gain),
            (tile[0][V_K:V_K + 1, 0:HD], swa_k_gain), (tile[0][V_K:V_K + 1, HD:P], swa_k_gain),
            (tile[1][0:TAPS * 4, 0:P], cf_conv_w.rearrange("l k (c p) -> (l k c) p", p=P)),
        ]
        other_loads = [
            (tile[7][:, 512:1024].rearrange("p (g n) -> p g n", g=4), pool_w.rearrange("l g c d -> c (l g) d")),
            (tile[6][:, 0:512].rearrange("p (h n) -> p h n", h=4), sgu_w.rearrange("l h t s -> t (l h) s")),
            (tile[5][:, 0:512].rearrange("p (t n) -> p t n", t=T), p.rearrange("l b (t p) n -> p (l b t) n", p=P)),
            (tile[4][0:32, 896:928], rel_bias), (tile[4][0:33, 0:384], buckets),
            (big[:, 0:512], sgu_ln_g.rearrange("l h d -> l (h d)").partition_broadcast(P)),
            (big[:, 512:1024], sgu_ln_b.rearrange("l h d -> l (h d)").partition_broadcast(P)),
            (sinks[:], swa_sinks.partition_broadcast(P)),
            (first16[:].rearrange("p g t -> p (g t)"), counts.partition_broadcast(P)),
        ]

        def conv_operands(lag, f):
            col = 4 * (TAPS - 1 - lag) + f
            return feat(0)[:, f, 0:S - lag], cw[:, col:col + 1], vec[:, V_CB + f:V_CB + f + 1]

        block = ctx.enter_context(nc.Block())

        @block.sync
        def _(sp_):
            def load(s, view, k, col, lap=ONCE):
                if s >= RAW:
                    sp_.wait_ge(lo_ready, s - RAW + 1 + 8 * lap.oct)
                sp_.dma_start(w_raw[:, s % RAW], view[:, bass.ds(k, CK), bass.ds(col, CW)]).then_inc(
                    raw_in[s % RAW], 16)

            for j in range(NG):
                sp_.dma_start(resid[:, :, CW * j:CW * (j + 1)], x_v[:, :, CW * j:CW * (j + 1)]).then_inc(x_in[j], 16)
                for c in (2 * j, 2 * j + 1):
                    load(c, win_v, CK * c, CW * IN_ORDER[0])
            for dst, src in small_loads:
                sp_.dma_start(dst, src).then_inc(params_in, 16)
            for u in range(1, 8):
                for c in range(8):
                    load(START[u] + c, win_v, CK * c, CW * IN_ORDER[u])
            for j in range(NG):
                load(START[PROJ_UNIT + j], wpp_v, 0, CW * j)
            for j in range(NG):
                for c in range(8):
                    load(START[OUT_UNIT + j] + c, wout_v, OUT_ROWS[c], CW * j)

            def load_pair(s, col, lap=ONCE):
                for c in range(8):
                    load(s + c, wg_v, CK * c, col, lap)
                for c in range(8):
                    load(s + 8 + c, wu_v, CK * c, col, lap)

            load_pair(START[FFN_UNIT], 0)
            with sp_.Fori(0, 2) as r:
                with sp_.Fori(0, 3) as j:
                    load_pair(START[FFN_UNIT + 2], (r * 4 + j) * CW + CW, Lap.at(r, j))
                for d in range(4):
                    for c in range(8):
                        load(START[FFN_UNIT + 8 + d] + c, wd_v, r * KT + CK * c, CW * d, Lap.at(r))
                load_pair(START[FFN_UNIT + 12], r * (4 * CW) + 4 * CW, Lap.at(r))
            base = FFN_UNIT + 26
            with sp_.Fori(0, 2) as j:
                load_pair(START[base], j * CW + 9 * CW, Lap(oct=2 * j))
            for d in range(4):
                for c in range(6):
                    load(START[base + 4 + d] + c, wd_v, 2 * KT + CK * c, CW * d)

            for j in range(NG):
                for c in range(8):
                    load(START[PLE_UNIT + j] + c, wpg_v, CK * c, CW * j)
            for j, col in enumerate(SWA_ORDER):
                for c in range(8):
                    load(START[SWA_UNIT + j] + c, swi_v, CK * c, CW * col)
            for j in range(NG):
                for c in range(8):
                    load(START[SO_UNIT + j] + c, swo_v, CK * c, CW * j)
            for j in range(NG - 1):
                wait_left(sp_, SO_UNIT + j)
                sp_.dma_start(out_v[:, :, CW * j:CW * (j + 1)], resid[:, :, CW * j:CW * (j + 1)]).then_inc(stored, 16)
            for t in range(T):
                sp_.wait_ge(last_sums, t + 1)
                sp_.dma_start(out_v[:, t, 3 * CW:], resid[:, t, 3 * CW:]).then_inc(stored, 16)
            sp_.wait_ge(stored, 16 * (NG - 1 + T))

        @block.gpsimd
        def _(pool):
            pool.memset(ident[:], 0.0).then_inc(consts, 1)
            pool.memset(flip[:], 0.0).then_inc(consts, 1)
            pool.memset(minus_half[:], -0.5).then_inc(consts, 1)
            pool.wait_ge(consts, 3)
            pool.memset(tile[4][32:33, 896:928], 1.0).then_inc(consts, 1)
            pool.wait_ge(consts, 4)
            pool.affine_select(out=ident[:], in_=ident[:], compare_op=ALU.not_equal, fill=1.0, base=0,
                               pattern=[[-1, P]], channel_multiplier=1).then_inc(consts, 1)
            pool.affine_select(out=flip[:], in_=flip[:], compare_op=ALU.not_equal, fill=1.0, base=1 - P,
                               pattern=[[1, P]], channel_multiplier=1).then_inc(consts, 1)
            pool.wait_ge(x_in[1], 16)
            for dst, src in other_loads:
                pool.dma_start(dst, src).then_inc(late_in, 16)
            pool.wait_ge(late_in, 16 * len(other_loads))
            causal = tile[6][:, 0:512].rearrange("p (h n) -> p h n", h=4)
            pool.affine_select(out=causal, in_=causal, compare_op=ALU.is_ge, fill=0.0, base=0,
                               pattern=[[0, 4], [-1, P]], channel_multiplier=1).then_inc(masked, 1)

            def rsqrt(k, src, n, scale):
                pool.wait_ge(want, k + 1)
                pool.tensor_scalar(eps_ms[:, k, 0:n], src, scale, EPS, ALU.mult, ALU.add).then_inc(eps_done, 1)
                pool.wait_ge(eps_done, k + 1)
                pool.tensor_tensor(rs[:, k, 0:n], eps_ms[:, k, 0:n], minus_half[:, 0:n], ALU.pow).then_inc(got, 1)

            rsqrt(R_X, ms[:, R_X, 0:T], T, 1.0 / D)
            pool.wait_ge(bias_sb, 1)
            pool.dma_start(bias_rows, tile[4][0:32, 512:896]).then_inc(bias_out, 16)
            wait_half_left(pool, H_HC + 1)
            for lag in range(TAPS):
                dst, (src, w_, bias) = feat(1)[:, 3, lag:S], conv_operands(lag, 3)
                if lag == 0:
                    pool.tensor_scalar(dst, src, w_, bias, ALU.mult, ALU.add).then_inc(conv_pool, 1)
                    continue
                term = conv_term[:, lag % 2, 0:S - lag]
                pool.tensor_scalar(term, src, w_, None, ALU.mult).then_inc(conv_terms, 1)
                pool.wait_ge(conv_terms, lag)
                pool.wait_ge(conv_pool, lag)
                pool.tensor_tensor(dst, dst, term, ALU.add).then_inc(conv_pool, 1)
            rsqrt(R_SGU, mv[:, :, 1], 8, 1.0)
            rsqrt(R_CONF, cmv[:, :, 1], T, 1.0)
            pool.wait_ge(sgu_ready, 1)
            pool.dma_start(big[:, :], final_norm_g.rearrange("(l n) -> l n", l=1).partition_broadcast(P)).then_inc(bias_in, 16)
            for k in (R_FFN, R_PLE, R_FIN):
                rsqrt(k, ms[:, k, 0:T], T, 1.0 / D)
            rsqrt(R_SWA, ssq_x1[:], T, 1.0 / D)

            def load_bias(g):
                src = bass.AP(bias_rows.tensor, g * HG * 3 * P, [[1, P], [3 * P, HG], [1, 2 * P]])
                pool.dma_start(big[:].rearrange("p (h n) -> p h n", h=HG), src).then_inc(bias_in, 16)

            pool.wait_ge(x1_ready, 1)
            pool.wait_ge(bias_out, 16)
            load_bias(0)
            rsqrt(R_K, ms[:, R_K, 0:8], 8, 1.0 / HD)
            for g in range(4):
                wait_left(pool, SWA_UNIT + 1 + g)
                pool.tensor_tensor(tile[5][:], tile[1][:], tile[1][:], ALU.mult).then_inc(q_squares, 1)
                if g:
                    pool.wait_ge(scored, 3 * g)
                    load_bias(g)
                rsqrt(R_Q + g, ms[:, R_Q + g, :], 16, 1.0 / HD)

        @block.scalar
        def _(act):
            def split(s, lap=ONCE):
                act.wait_ge(raw_in[s % RAW], 16 * (s // RAW + 1) + 16 * lap.oct)
                if s >= SPL:
                    act.wait_ge(used, s - SPL + 1 + 8 * lap.oct)
                act.activation(w_hi[:, s % SPL], w_raw[:, s % RAW], ACT.Copy).then_inc(hi_ready, 1)

            def take(u, dst, func, scale, lap=ONCE):
                wait_unit(act, u, lap)
                for t in range(T):
                    s_ = scale if isinstance(scale, float) else scale[:, t:t + 1]
                    last = act.activation(dst[:, t], acc[u % 2][t][:], func, scale=s_)
                last.then_inc(left["a"], 1)

            def high(h, dst, gains=None, lap=ONCE):
                for i in range(2):
                    wait_half(act, h + i, lap)
                    if gains is None:
                        last = act.activation(dst[:, 2 * i:2 * i + 2], half_tile(h + i), ACT.Copy)
                    else:
                        for k in range(2):
                            last = act.activation(dst[:, 2 * i + k], half_tile(h + i)[:, k], ACT.Copy,
                                                  scale=gains[:, 2 * i + k:2 * i + k + 1])
                    last.then_inc(feat_hi, 1)

            def copy(h, dst, scale=1.0):
                for i in range(2):
                    wait_half(act, h + i)
                    act.activation(dst[:, 512 * i:512 * (i + 1)], tp[(h + i) % 2][:], ACT.Copy,
                                   scale=scale).then_inc(tp_left["a"], 1)

            def square(row, j, junk=6):
                if row or j:
                    act.wait_ge(squares, 8 * row + 2 * j)
                for t in range(T):
                    act.activation(tok(junk)[:, t], resid[:, t, CW * j:CW * (j + 1)], ACT.Square,
                                   accum_out=ssq[:, row, t, j:j + 1]).then_inc(squares, 1)

            rx = rs[:, R_X]
            act.dma_start(tile[0][V_MIX:V_MIX + KT, 0:P], norm_mix_g.rearrange("l (k p) -> (l k) p", p=P)).then_inc(mix_in, 16)
            act.wait_ge(consts, 3)
            act.activation(rden[:, 11, :], minus_half[:, 0:8], ACT.Copy)
            for u in range(8):
                for c in range(8):
                    s = START[u] + c
                    if s == 0:
                        split(s)
                        wait_half_left(act, H_MIX)
                    if u == 0 and c % 2 == 0:
                        high(H_X + c, yh[:, 2 * c:2 * c + 4], vec[:, V_MIX + 2 * c:V_MIX + 2 * c + 4])
                    if s:
                        split(s)
                    if u == 0 and c >= 4:
                        square(0, c - 4, junk=2)
                    if (u, c) == (1, 3):
                        act.wait_ge(got, R_X + 1)
                        take(U_G, tok(2), ACT.Sigmoid, rx)
                    if (u, c) == (1, 5):
                        wait_half(act, H_INIT + 1)
                        act.activation(hh[:, 12:14], half_tile(H_INIT + 1), ACT.Copy).then_inc(feat_hi, 1)
                        act.wait_ge(bias_psum, 1)
                        act.activation(tile[4][0:32, 512:896], sp[0][0:32, 0:384], ACT.Copy).then_inc(bias_sb, 1)
                    if (u, c) == (2, 7):
                        copy(H_HC, tile[0])
                    if (u, c) == (3, 3):
                        wait_left(act, U_A)
                        take(U_H, tok(2), ACT.Copy, rx)
                    if (u, c) == (4, 7):
                        act.wait_ge(bias_out, 16)
                        copy(H_SC, tile[4])
                    if (u, c) == (5, 3):
                        take(U_BG, tok(2), ACT.Copy, rx)
                    if (u, c) == (6, 1):
                        wait_half_left(act, H_BG + 1)
                        act.activation(hh[:, 0:4], feat(5), ACT.Copy).then_inc(mix_hi, 1)
                    if (u, c) == (6, 3):
                        take(U_D, tok(3), ACT.Copy, rx)
                    if (u, c) == (6, 7):
                        copy(H_PZ, tile[4])
                    if (u, c) == (7, 3):
                        take(U_V, tok(2), ACT.Gelu_apprx_tanh, rx)
                    if (u, c) == (7, 5):
                        high(H_PO, hh[:, 4:8], vec[:, V_PS:V_PS + 4])
            wide_v = wide[:]
            for j in range(4):
                split(START[PROJ_UNIT + j])
            take(U_U, tok(3), ACT.Gelu_apprx_tanh, rx)
            take(PROJ_UNIT, wide_v[:, :, 0:CW], ACT.Copy, 1.0)
            for j in range(NG):
                for c in range(8):
                    split(START[OUT_UNIT + j] + c)
                    if j == 0 and c < 3:
                        take(PROJ_UNIT + 1 + c, wide_v[:, :, CW * (c + 1):CW * (c + 2)], ACT.Copy, 1.0)
                    if (j, c) == (0, 1):
                        wait_half_left(act, H_PO + 1)
                        for i in range(2):
                            wait_half(act, H_CN + i)
                            for k in range(2):
                                f = 2 * i + k
                                last = act.activation(feat(6)[:, f], half_tile(H_CN + i)[:, k], ACT.Silu,
                                                      bias=vec[:, V_LB + f:V_LB + f + 1],
                                                      scale=vec[:, V_LG + f:V_LG + f + 1])
                            last.then_inc(tp_left["a"], 1)
                        wait_half_left(act, H_CN + 1)
                        act.activation(hh[:, 12:16], feat(6), ACT.Copy).then_inc(mix_hi, 1)
                    if (j, c) == (0, 3):
                        high(H_OA, hh[:, 8:12])
                    if j and c == 4:
                        wait_left(act, OUT_UNIT + j - 1)
                        if j == 1:
                            act.wait_ge(mix_ready, 2)
                        square(1, j - 1)
                    if j and c == 5:
                        high(H_FFN + 2 * (j - 1), yh[:, 4 * j - 4:4 * j], vec[:, V_FFN + 4 * j - 4:V_FFN + 4 * j])

            rf = rs[:, R_FFN]

            def pair(s, u, lap, kt=None, first=False, fresh=False):
                for c in range(16):
                    split(s + c, lap)
                    if first and c == 4:
                        wait_left(act, OUT_UNIT + 3)
                        square(1, 3)
                    if first and c == 5:
                        high(H_FFN + 6, yh[:, 12:16], vec[:, V_FFN + 12:V_FFN + 16])
                    if kt is not None and c == 5:
                        high(H_HID, hh[:, bass.ds(kt, 4)], None, lap)
                    if c == 11:
                        if first:
                            act.wait_ge(got, R_FFN + 1)
                        else:
                            wait_left(act, u - 1, lap)
                        take(u, tok(0), ACT.Silu, rf, lap)

            pair(START[FFN_UNIT], FFN_UNIT, ONCE, first=True)
            with act.Fori(0, 2) as r:
                with act.Fori(0, 3) as j:
                    pair(START[FFN_UNIT + 2], FFN_UNIT + 2, Lap.at(r, j), kt=j * 4)
                for d in range(4):
                    for c in range(8):
                        split(START[FFN_UNIT + 8 + d] + c, Lap.at(r))
                        if (d, c) == (0, 5):
                            high(H_HID + 6, hh[:, 12:16], None, Lap.at(r))
                pair(START[FFN_UNIT + 12], FFN_UNIT + 12, Lap.at(r))
            base = FFN_UNIT + 26

            with act.Fori(0, 2) as j:
                lap = Lap(2 * j, j, j, 2 * j)
                for c in range(16):
                    split(START[base] + c, lap)
                    if c == 5:
                        high(H_HID + 16, hh[:, bass.ds(j * 4, 4)], None, lap)
                    if c == 11:
                        wait_left(act, base - 1, lap)
                        take(base, tok(0), ACT.Silu, rf, lap)
            for d in range(4):
                for c in range(6):
                    split(START[base + 4 + d] + c)
                    if (d, c) == (0, 5):
                        high(H_HID + 20, hh[:, 8:12])
                    if d and c == 4:
                        wait_left(act, base + 4 + d - 1)
                        square(2, d - 1)
                    if d and c == 5:
                        high(H_PLE + 2 * (d - 1), yh[:, 4 * d - 4:4 * d], vec[:, V_PLE + 4 * d - 4:V_PLE + 4 * d])
            rp = rs[:, R_PLE]
            for j in range(NG):
                for c in range(8):
                    split(START[PLE_UNIT + j] + c)
                    if j == 0 and c == 4:
                        wait_left(act, PLE_UNIT - 1)
                        square(2, 3)
                    if j == 0 and c == 5:
                        high(H_PLE + 6, yh[:, 12:16], vec[:, V_PLE + 12:V_PLE + 16])
                    if j and c == 3:
                        if j == 1:
                            act.wait_ge(got, R_PLE + 1)
                        else:
                            act.wait_ge(x1_ready, j - 1)
                        take(PLE_UNIT + j - 1, tok(0), ACT.Sigmoid, rp)
                    if j and c == 4:
                        act.wait_ge(x1_ready, j)
                        square(3, j - 1)
                    if j and c == 5:
                        high(H_SWA + 2 * (j - 1), hh[:, 4 * j - 4:4 * j], gfs[:, 4 * j - 4:4 * j])
            def exp(g, r):
                n = 3 * g + r
                _, h0, nh, nk = ROUNDS[r]
                act.wait_ge(smax, n + 1)
                sv = tile[(2, 6)[n % 2]][:].rearrange("p (h n) -> p h n", h=nh)
                for i in range(nh):
                    act.activation(sv[:, i], sv[:, i], ACT.Exp, bias=negm[:, n, i:i + 1],
                                   accum_out=ssum[:, n, i:i + 1])
                act.activation(ssink[:, n, 0:nh], ssink[:, n, 0:nh], ACT.Exp).then_inc(expd, 1)

            for v in range(9):
                for c in range(8):
                    split(START[SWA_UNIT + v] + c)
                    if (v, c) == (0, 3):
                        act.wait_ge(x1_ready, 3)
                        take(PLE_UNIT + 3, tok(0), ACT.Sigmoid, rp)
                    if (v, c) == (0, 4):
                        act.wait_ge(x1_ready, 4)
                        square(3, 3)
                    if (v, c) == (0, 5):
                        high(H_SWA + 6, hh[:, 12:16], gfs[:, 12:16])
                    if (v, c) in ((0, 7), (1, 0)):
                        t = v
                        act.wait_ge(x1_ready, 5)
                        act.activation(wide[:, t], resid[:, t], ACT.Square,
                                       accum_out=ssq_x1[:, t:t + 1]).then_inc(squares, 1)
                    if (v, c) == (1, 3):
                        act.wait_ge(prod, 2)
                        take(SWA_UNIT, tok(0), ACT.Copy, rr)
                    if (v, c) == (1, 7):
                        act.wait_ge(kv_flipped, 1)
                        for t in range(T):
                            last = act.activation(tok(0)[:, t], sp[t][:], ACT.Copy)
                        last.then_inc(kv_ready, 1)
                    if (v, c) == (2, 6):
                        copy(H_K, tile[3])
                    if c == 0 and 3 <= v <= 6:
                        copy(H_Q[v - 3], tile[4], gqk[:, 0:1])
                    if c == 0 and v >= 7:
                        high(H_OG[v - 7], yh[:, 4 * (v - 7):4 * (v - 7) + 4])
                    if c == 2 and 4 <= v <= 7:
                        copy(H_PT[v - 4, 2], tile[7])
                    if c == 2 and 3 <= v <= 6:
                        exp(v - 3, 0)
                    if c == 3 and 2 <= v <= 5:
                        take(SWA_UNIT + v - 1, tok(1), ACT.Copy, rr)
                    if c == 3 and v >= 6:
                        if v > 6:
                            act.wait_ge(og_ready, v - 6)
                        take(SWA_UNIT + v - 1, tok(1), ACT.Silu, rr)
                    if c == 4 and 3 <= v <= 6:
                        exp(v - 3, 1)
                    if c == 5 and 3 <= v <= 6:
                        copy(H_PT[v - 3, 0], tile[7])
                    if c == 6 and 3 <= v <= 6:
                        exp(v - 3, 2)
                    if c == 7 and 3 <= v <= 6:
                        copy(H_PT[v - 3, 1], tile[7])
            for j in range(NG):
                for c in range(8):
                    split(START[SO_UNIT + j] + c)
                    if (j, c) == (0, 0):
                        high(H_OG[2], yh[:, 8:12])
                    if (j, c) == (0, 3):
                        act.wait_ge(og_ready, 3)
                        take(SO_UNIT - 1, tok(1), ACT.Silu, rr)
                    if (j, c) == (0, 5):
                        high(H_OG[3], yh[:, 12:16])

        @block.vector
        def _(dve):
            steps = [0]

            def step(ins):
                steps[0] += 1
                ins.then_inc(vstep, 1)
                dve.wait_ge(vstep, steps[0])

            def split(s, lap=ONCE):
                dve.wait_ge(hi_ready, s + 1 + 8 * lap.oct)
                dve.tensor_tensor(w_lo[:, s % SPL], w_raw[:, s % RAW], w_hi[:, s % SPL].bitcast(F32),
                                  ALU.subtract).then_inc(lo_ready, 1)

            def low(h, dst, hi, gains=None, lap=ONCE, halves=2):
                for i in range(halves):
                    dve.wait_ge(feat_hi, hi_count(h + i) + lap.h)
                    if gains is None:
                        last = dve.tensor_tensor(dst[:, 2 * i:2 * i + 2], half_tile(h + i),
                                                 hi[:, 2 * i:2 * i + 2].bitcast(F32), ALU.subtract)
                    else:
                        for k in range(2):
                            f = 2 * i + k
                            last = dve.scalar_tensor_tensor(dst[:, f], half_tile(h + i)[:, k], gains[:, f:f + 1],
                                                            hi[:, f].bitcast(F32), ALU.mult, ALU.subtract)
                    last.then_inc(tp_left["d"], 1)

            def add_resid(u, j, lap=ONCE):
                wait_unit(dve, u, lap)
                for t in range(T):
                    cols = resid[:, t, CW * j:CW * (j + 1)]
                    last = dve.tensor_tensor(cols, acc[u % 2][t][:], cols, ALU.add)
                last.then_inc(left["d"], 1)

            def request(k, count):
                dve.wait_ge(squares, count)
                dve.tensor_reduce(ms[:, k, 0:T], ssq[:, {R_X: 0, R_FFN: 1, R_PLE: 2, R_FIN: 3}[k]], AX,
                                  ALU.add).then_inc(want, 1)

            rx = rs[:, R_X]
            wait_half(dve, H_MIX)
            dve.tensor_copy(vec[:, V_MIX:V_MIX + KT], tp[H_MIX % 2][:, 0:KT]).then_inc(tp_left["d"], 1)

            def conv_steps(lag):
                for f in range(3):
                    dst, (src, w_, bias) = feat(1)[:, f, lag:S], conv_operands(lag, f)
                    if lag == 0:
                        dve.tensor_scalar(dst, src, w_, bias, ALU.mult, ALU.add).then_inc(conv, 1)
                    else:
                        dve.wait_ge(conv, 3 * (lag - 1) + f + 1)
                        dve.scalar_tensor_tensor(dst, src, w_, dst, ALU.mult, ALU.add).then_inc(conv, 1)

            for u in range(8):
                for c in range(8):
                    s = START[u] + c
                    if s == 0:
                        split(s)
                        wait_half_left(dve, H_MIX)
                    if u == 0 and c % 2 == 0:
                        low(H_X + c, yl[:, 2 * c:2 * c + 4], yh[:, 2 * c:2 * c + 4],
                            vec[:, V_MIX + 2 * c:V_MIX + 2 * c + 4])
                    if s:
                        split(s)
                    if (u, c) == (1, 0):
                        request(R_X, 8)
                    if (u, c) == (1, 3):
                        wait_half(dve, H_VEC)
                        dve.tensor_copy(vec[:, KT:114], tp[H_VEC % 2][:, KT:114])
                        dve.tensor_copy(cw[:], tp[H_VEC % 2][:, P:P + TAPS * 4]).then_inc(tp_left["d"], 1)
                        wait_half_left(dve, H_VEC)
                        dve.tensor_tensor(gfs[:], vec[:, V_FIN:V_FIN + KT], vec[:, V_SWA:V_SWA + KT],
                                          ALU.mult).then_inc(prod, 1)
                        dve.scalar_tensor_tensor(gqk[:], vec[:, V_Q:V_Q + 1], HD ** -0.5, vec[:, V_K:V_K + 1],
                                                 ALU.mult, ALU.mult)
                        dve.wait_ge(late_in, 16 * len(other_loads))
                        dve.reciprocal(rcount[:], first16[:])
                    if (u, c) == (1, 4):
                        wait_half(dve, H_INIT)
                        dve.tensor_copy(tile[7][:, 0:512], tp[H_INIT % 2][:]).then_inc(tp_left["d"], 1)
                    if (u, c) == (1, 5):
                        low(H_INIT + 1, hl[:, 12:14], hh[:, 12:14], halves=1)
                    if (u, c) == (2, 3):
                        wait_left(dve, U_G)
                        wait_unit(dve, U_A)
                        for t in range(T):
                            last = dve.scalar_tensor_tensor(tok(3)[:, t], acc[U_A % 2][t][:], rx[:, t:t + 1],
                                                            tok(2)[:, t], ALU.mult, ALU.mult)
                        last.then_inc(left["d"], 1)
                    if s >= 24 and s not in BUSY:
                        if s == 24:
                            wait_half_left(dve, H_HC + 1)
                        conv_steps(sum(1 for i in range(24, s) if i not in BUSY))
                    if (u, c) == (4, 3):
                        wait_left(dve, U_H)
                        wait_unit(dve, U_CG)
                        for t in range(T):
                            last = dve.scalar_tensor_tensor(tok(3)[:, t], acc[U_CG % 2][t][:], rx[:, t:t + 1],
                                                            tok(2)[:, t], ALU.mult, ALU.mult)
                        last.then_inc(left["d"], 1)
                    if (u, c) == (5, 0):
                        wait_half_left(dve, H_SC + 1)
                        for lag in range(3):
                            for f in range(4):
                                col = V_SC + 4 * (2 - lag) + f
                                src, dst = feat(4)[:, f, 0:S - lag], feat(5)[:, f, lag:S]
                                if lag == 0:
                                    last = dve.tensor_scalar(dst, src, vec[:, col:col + 1], None, ALU.mult)
                                else:
                                    last = dve.scalar_tensor_tensor(dst, src, vec[:, col:col + 1], dst, ALU.mult, ALU.add)
                            step(last)
                    if (u, c) == (5, 7):
                        for i in range(2):
                            wait_half(dve, H_BG + i)
                            part = tile[5][:, 512 * i:512 * (i + 1)]
                            dve.tensor_tensor(part, part, tp[(H_BG + i) % 2][:], ALU.mult).then_inc(tp_left["d"], 1)
                    if (u, c) == (6, 1):
                        dve.wait_ge(mix_hi, 1)
                        dve.tensor_tensor(hl[:, 0:4], feat(5), hh[:, 0:4].bitcast(F32), ALU.subtract).then_inc(mix_ready, 1)
                    if (u, c) == (7, 0):
                        wait_half_left(dve, H_PZ + 1)
                        z, a, b = feat(4), feat(5), feat(6)
                        dve.wait_ge(mix_ready, 1)
                        for f0, src, dst in ((0, z, a), (1, a, b), (2, b, a), (3, a, b)):
                            lag = 1 << f0
                            dve.tensor_copy(dst[:, f0:4, 0:lag], src[:, f0:4, 0:lag])
                            step(dve.tensor_tensor(dst[:, f0:4, lag:S], src[:, f0:4, lag:S], src[:, f0:4, 0:S - lag], ALU.add))
                    if (u, c) == (7, 1):
                        for f, w in enumerate(WINDOWS):
                            last = dve.tensor_tensor(first16[:, f], (a, b)[f % 2][:, f, 0:16], rcount[:, f], ALU.mult)
                        step(last)
                        for f, w in enumerate(WINDOWS):
                            y_ = (a, b)[f % 2][:, f]
                            last = dve.scalar_tensor_tensor(y_, y_, 1.0 / w, z[:, f], ALU.mult, ALU.subtract)
                        step(last)
                        for f in range(4):
                            last = dve.tensor_tensor((a, b)[f % 2][:, f, 0:16], first16[:, f], z[:, f, 0:16], ALU.subtract)
                        last.then_inc(pooled, 1)
                    if (u, c) == (7, 4):
                        wait_left(dve, U_V)
                        vh = tile[2][:].rearrange("p (i n) -> p i n", i=8)
                        for i in range(8):
                            last = dve.bn_stats(st[:, i], vh[:, i])
                        step(last)
                        for i in range(8):
                            last = dve.bn_aggr(mv[:, i], st[:, i])
                        last.then_inc(want, 1)
                    if (u, c) == (7, 5):
                        low(H_PO, hl[:, 4:8], hh[:, 4:8], vec[:, V_PS:V_PS + 4])
                    if (u, c) == (7, 6):
                        dve.wait_ge(got, R_SGU + 1)
                        for i in range(8):
                            last = dve.tensor_scalar(vh[:, i], vh[:, i], mv[:, i, 0:1], rs[:, R_SGU, i:i + 1],
                                                     ALU.subtract, ALU.mult)
                        step(last)
                    if (u, c) == (7, 7):
                        for t in range(T):
                            last = dve.tensor_tensor(tok(2)[:, t], tok(2)[:, t], big[:, 0:512], ALU.mult)
                        step(last)
                        for t in range(T):
                            last = dve.tensor_tensor(tok(2)[:, t], tok(2)[:, t], big[:, 512:1024], ALU.add)
                        last.then_inc(sgu_ready, 1)
            for j in range(4):
                split(START[PROJ_UNIT + j])
            for t in range(T):
                wait_half(dve, H_CB + t)
                last = dve.bn_stats(cst[:, t], tp[(H_CB + t) % 2][:])
            step(last)
            for t in range(T):
                last = dve.bn_aggr(cmv[:, t], cst[:, t])
            last.then_inc(want, 1)
            dve.wait_ge(got, R_CONF + 1)
            for t in range(T):
                dve.tensor_scalar(tok(4)[:, t], tp[(H_CB + t) % 2][:], cmv[:, t, 0:1], rs[:, R_CONF, t:t + 1],
                                  ALU.subtract, ALU.mult).then_inc(tp_left["d"], 1)
            for j in range(NG):
                for c in range(8):
                    split(START[OUT_UNIT + j] + c)
                    if (j, c) == (0, 0):
                        wait_left(dve, U_U)
                        dve.wait_ge(sgu_sum, 1)
                        for t in range(T):
                            for h in range(4):
                                cols = slice(P * h, P * (h + 1))
                                last = dve.scalar_tensor_tensor(tok(5)[:, t, cols], sp[t][:, cols],
                                                                vec[:, V_SB + h:V_SB + h + 1], tok(3)[:, t, cols],
                                                                ALU.add, ALU.mult)
                        last.then_inc(oa_ready, 1)
                    if (j, c) == (0, 2):
                        dve.wait_ge(mix_hi, 2)
                        dve.tensor_tensor(hl[:, 12:16], feat(6), hh[:, 12:16].bitcast(F32), ALU.subtract).then_inc(mix_ready, 1)
                    if (j, c) == (0, 3):
                        low(H_OA, hl[:, 8:12], hh[:, 8:12])
                    if j and c == 3:
                        add_resid(OUT_UNIT + j - 1, j - 1)
                    if j and c == 5:
                        q = slice(4 * j - 4, 4 * j)
                        low(H_FFN + 2 * (j - 1), yl[:, q], yh[:, q], vec[:, V_FFN + 4 * j - 4:V_FFN + 4 * j])

            rf = rs[:, R_FFN]

            def hidden(u, lap=ONCE):
                wait_left(dve, u, lap)
                wait_unit(dve, u + 1, lap)
                for t in range(T):
                    last = dve.scalar_tensor_tensor(tok(1)[:, t], acc[(u + 1) % 2][t][:], rf[:, t:t + 1],
                                                    tok(0)[:, t], ALU.mult, ALU.mult)
                last.then_inc(left["d"], 1)

            def pair(s, lap, before, half=None, kt=None, first=False):
                for c in range(16):
                    split(s + c, lap)
                    if c == 3:
                        before()
                    if first and c == 5:
                        low(H_FFN + 6, yl[:, 12:16], yh[:, 12:16], vec[:, V_FFN + 12:V_FFN + 16])
                        request(R_FFN, 16)
                    if kt is not None and c == 5:
                        low(half, hl[:, bass.ds(kt, 4)], hh[:, bass.ds(kt, 4)], None, lap)

            pair(START[FFN_UNIT], ONCE, lambda: add_resid(OUT_UNIT + 3, 3), first=True)
            with dve.Fori(0, 2) as r:
                with dve.Fori(0, 3) as j:
                    lap = Lap.at(r, j)
                    pair(START[FFN_UNIT + 2], lap, lambda: hidden(FFN_UNIT, lap), H_HID, j * 4)
                lap = Lap.at(r)
                for d in range(4):
                    for c in range(8):
                        split(START[FFN_UNIT + 8 + d] + c, lap)
                        if (d, c) == (0, 3):
                            hidden(FFN_UNIT + 6, lap)
                        if (d, c) == (0, 5):
                            low(H_HID + 6, hl[:, 12:16], hh[:, 12:16], None, lap)
                        if d and c == 3:
                            add_resid(FFN_UNIT + 8 + d - 1, d - 1, lap)
                pair(START[FFN_UNIT + 12], lap, lambda: add_resid(FFN_UNIT + 11, 3, lap))
            base = FFN_UNIT + 26
            with dve.Fori(0, 2) as j:
                lap = Lap(2 * j, j, j, 2 * j)
                pair(START[base], lap, lambda: hidden(base - 2, lap), H_HID + 16, j * 4)
            for d in range(4):
                for c in range(6):
                    split(START[base + 4 + d] + c)
                    if (d, c) == (0, 3):
                        hidden(base + 2)
                    if (d, c) == (0, 5):
                        low(H_HID + 20, hl[:, 8:12], hh[:, 8:12])
                    if d and c == 3:
                        add_resid(base + 4 + d - 1, d - 1)
                    if d and c == 5:
                        q = slice(4 * d - 4, 4 * d)
                        low(H_PLE + 2 * (d - 1), yl[:, q], yh[:, q], vec[:, V_PLE + 4 * d - 4:V_PLE + 4 * d])

            def add_gated(j):
                wait_left(dve, PLE_UNIT + j)
                step(dve.tensor_tensor(tok(0), tok(0), wide[:, :, CW * j:CW * (j + 1)], ALU.mult))
                cols = resid[:, :, CW * j:CW * (j + 1)]
                dve.tensor_tensor(cols, cols, tok(0), ALU.add).then_inc(x1_ready, 1)

            for j in range(NG):
                for c in range(8):
                    split(START[PLE_UNIT + j] + c)
                    if j == 0 and c == 3:
                        add_resid(PLE_UNIT - 1, 3)
                    if j == 0 and c == 5:
                        low(H_PLE + 6, yl[:, 12:16], yh[:, 12:16], vec[:, V_PLE + 12:V_PLE + 16])
                        request(R_PLE, 24)
                    if j and c == 3:
                        add_gated(j - 1)
                    if j and c == 5:
                        q = slice(4 * j - 4, 4 * j)
                        low(H_SWA + 2 * (j - 1), hl[:, q], hh[:, q], gfs[:, q])

            def query_stats(g):
                dve.wait_ge(q_squares, g + 1)
                dve.tensor_reduce(ms[:, R_Q + g, :], tile[5][:].rearrange("p (h n) -> p h n", n=HD), AX,
                                  ALU.add).then_inc(want, 1)

            def softmax_max(g, r):
                n = 3 * g + r
                t, h0, nh, nk = ROUNDS[r]
                dve.wait_ge(scores, n + 1)
                if r == 0:
                    dve.wait_ge(got, R_Q + g + 1)
                    dve.wait_ge(bias_in, 16 * (g + 2))
                w = P * nk
                sv = tile[(2, 6)[n % 2]][:].rearrange("p (h n) -> p h n", h=nh)
                bias = big[:].rearrange("p (h n) -> p h n", h=HG)
                for i in range(nh):
                    src = sp[i % 2][:, w * (i // 2):w * (i // 2) + w]
                    h = h0 + i
                    last = dve.scalar_tensor_tensor(sv[:, i], src, rs[:, R_Q + g, 8 * t + h:8 * t + h + 1],
                                                    bias[:, h, 0:w], ALU.mult, ALU.add)
                last.then_inc(scored, 1)
                dve.wait_ge(scored, n + 1)
                step(dve.tensor_reduce(smx[:, n, 0:nh], sv, AX, ALU.max))
                snk = sinks[:, HG * g + h0:HG * g + h0 + nh]
                step(dve.tensor_tensor(smx[:, n, 0:nh], smx[:, n, 0:nh], snk, ALU.max))
                dve.tensor_scalar(negm[:, n, 0:nh], smx[:, n, 0:nh], -1.0, None, ALU.mult)
                dve.tensor_tensor(ssink[:, n, 0:nh], snk, smx[:, n, 0:nh], ALU.subtract).then_inc(smax, 1)

            def weighted(g, r):
                n = 3 * g + r
                t, h0, nh, nk = ROUNDS[r]
                dve.wait_ge(expd, n + 1)
                step(dve.tensor_tensor(rden[:, n, 0:nh], ssum[:, n, 0:nh], ssink[:, n, 0:nh], ALU.add))
                step(dve.reciprocal(rden[:, n, 0:nh], rden[:, n, 0:nh]))
                h = H_PV[g, r]
                wait_half(dve, h)
                dst = wide[:, t, CW * g + HD * h0:CW * g + HD * (h0 + nh)].rearrange("p (h n) -> p h n", n=HD)
                src = tp[h % 2][:, 0:HD * nh].rearrange("p (h n) -> p h n", n=HD)
                by = rden[:, n, 0:nh].unsqueeze(2).to_broadcast([P, nh, HD])
                dve.tensor_tensor(dst, src, by, ALU.mult).then_inc(tp_left["d"], 1)

            def gated(g):
                wait_left(dve, SWA_UNIT + 5 + g)
                cols = wide[:, :, CW * g:CW * (g + 1)]
                if g == 3:
                    wait_half_left(dve, H_PV[3, 2])
                dve.tensor_tensor(cols, cols, tok(1), ALU.mult).then_inc(og_ready, 1)

            for v in range(9):
                for c in range(8):
                    split(START[SWA_UNIT + v] + c)
                    if (v, c) == (0, 3):
                        add_gated(3)
                    if (v, c) == (0, 5):
                        low(H_SWA + 6, hl[:, 12:16], hh[:, 12:16], gfs[:, 12:16])
                        request(R_FIN, 32)
                    if (v, c) == (0, 6):
                        dve.wait_ge(got, R_FIN + 1)
                        dve.wait_ge(bias_in, 16)
                        for t in range(T):
                            last = dve.scalar_tensor_tensor(resid[:, t], resid[:, t], rs[:, R_FIN, t:t + 1], big[:],
                                                            ALU.mult, ALU.mult)
                        last.then_inc(x1_ready, 1)
                    if (v, c) == (1, 1):
                        dve.wait_ge(squares, 34)
                        dve.engine_nop().then_inc(want, 1)
                    if (v, c) == (1, 2):
                        dve.wait_ge(got, R_SWA + 1)
                        dve.tensor_tensor(rr[:], rs[:, R_FIN, 0:T], rs[:, R_SWA, 0:T], ALU.mult).then_inc(prod, 1)
                    if (v, c) == (2, 0):
                        dve.wait_ge(kv_ready, 1)
                        kv = tok(0)[:, :, 0:256]
                        step(dve.tensor_tensor(tok(5)[:, :, 0:256], kv, kv, ALU.mult))
                        for t in range(T):
                            last = dve.tensor_reduce(ms[:, R_K, 4 * t:4 * t + 4],
                                                     tok(5)[:, t, 0:256].rearrange("p (h n) -> p h n", n=HD), AX, ALU.add)
                        last.then_inc(want, 1)
                    if (v, c) == (2, 1):
                        dve.wait_ge(got, R_K + 1)
                        for t in range(T):
                            k_ = tok(0)[:, t, 0:256].rearrange("p (h n) -> p h n", n=HD)
                            by = rs[:, R_K, 4 * t:4 * t + 4].unsqueeze(2).to_broadcast([P, 4, HD])
                            kd = tok(2)[:, t].rearrange("p (h d n) -> p h d n", h=4, d=2)
                            for d in range(2):
                                last = dve.tensor_tensor(kd[:, :, d], k_, by, ALU.mult)
                        last.then_inc(kd_ready, 1)
                    if c == 0 and v >= 7:
                        q = slice(4 * (v - 7), 4 * (v - 7) + 4)
                        low(H_OG[v - 7], yl[:, q], yh[:, q])
                    if c == 1 and 4 <= v <= 7:
                        weighted(v - 4, 1)
                    if c == 1 and 3 <= v <= 6:
                        softmax_max(v - 3, 0)
                    if c == 3 and 3 <= v <= 6:
                        softmax_max(v - 3, 1)
                    if c == 3 and 4 <= v <= 7:
                        weighted(v - 4, 2)
                    if c == 7 and 2 <= v <= 5:
                        query_stats(v - 2)
                    if c == 3 and v >= 6:
                        gated(v - 6)
                    if c == 5 and 3 <= v <= 6:
                        softmax_max(v - 3, 2)
                    if c == 6 and 3 <= v <= 6:
                        weighted(v - 3, 0)
            for j in range(NG):
                for c in range(8):
                    split(START[SO_UNIT + j] + c)
                    if (j, c) == (0, 0):
                        low(H_OG[2], yl[:, 8:12], yh[:, 8:12])
                    if (j, c) == (0, 3):
                        gated(3)
                    if (j, c) == (0, 5):
                        low(H_OG[3], yl[:, 12:16], yh[:, 12:16])
                    if j and c == 3:
                        add_resid(SO_UNIT + j - 1, j - 1)
            wait_unit(dve, SO_UNIT + 3)
            for t in range(T):
                cols = resid[:, t, 3 * CW:]
                dve.tensor_tensor(cols, acc[(SO_UNIT + 3) % 2][t][:], cols, ALU.add).then_inc(last_sums, 1)

        @block.tensor
        def _(pe):
            def chunk(s, u, c, xh, xl, lap=ONCE):
                if c == 0 and u >= 2:
                    wait_left(pe, u - 2, lap)
                pe.wait_ge(lo_ready, s + 1 + 8 * lap.oct)
                n = UNITS[u][0]
                for t in range(T):
                    for k in range(CK):
                        f = CK * c + k
                        dst, tk = acc[u % 2][t][:], slice(P * t, P * (t + 1))
                        pe.matmul(dst, xh[:, f, tk], w_lo[:, s % SPL, k], start=(f == 0), stop=False)
                        pe.matmul(dst, xh[:, f, tk], w_hi[:, s % SPL, k], start=False, stop=False)
                        last = pe.matmul(dst, xl[:, f, tk], w_hi[:, s % SPL, k], start=False,
                                         stop=(f == CK * n - 1))
                last.then_inc(used, 1)

            def free(h, lap=ONCE):
                if before(h) is not None:
                    wait_half_left(pe, before(h), lap)

            def to_features(h, src, lap=ONCE):
                for i in range(2):
                    free(h + i, lap)
                    for k in range(2):
                        for t in range(T):
                            f = 2 * i + k
                            last = pe.transpose(half_tile(h + i)[:, k, P * t:P * (t + 1)],
                                                src[:, t, P * f:P * (f + 1)], ident[:])
                    last.then_inc(tp_ready, 1)

            def blocks(h, src, n=8):
                for b in range(n):
                    i = b // 4
                    if b % 4 == 0:
                        free(h + i)
                    last = pe.transpose(tp[(h + i) % 2][:, P * (b % 4):P * (b % 4 + 1)], src(b), ident[:])
                    if b % 4 == 3:
                        last.then_inc(tp_ready, 1)

            pe.wait_ge(consts, 5)
            for _ in range(8):
                pe.matmul(acc[1][0][:, 0:P], ident[:], ident[:], start=True, stop=True)
            pe.wait_ge(mix_in, 16)
            pe.transpose(tp[H_MIX % 2][:, 0:KT], tile[0][0:KT, 0:P], ident[0:KT, 0:KT]).then_inc(tp_ready, 1)

            def turn_x(j):
                pe.wait_ge(x_in[j], 16)
                to_features(H_X + 2 * j, resid[:, :, CW * j:CW * (j + 1)])

            turn_x(0)
            for u in range(8):
                for c in range(8):
                    if u == 0 and c % 2 == 0:
                        if c in (2, 4):
                            turn_x(c // 2 + 1)
                        wait_half_left(pe, H_X + c + 1)
                    chunk(START[u] + c, u, c, yh, yl)
                    if (u, c) == (0, 0):
                        turn_x(1)
                    if (u, c) == (1, 0):
                        pe.wait_ge(consts, 6)
                        pe.wait_ge(params_in, 16 * len(small_loads))
                        free(H_VEC)
                        pe.transpose(tp[H_VEC % 2][:, 0:114], tile[0][0:114, 0:P], ident[0:114, 0:114])
                        pe.transpose(tp[H_VEC % 2][:, P:P + 124], tile[1][0:124, 0:P],
                                     ident[0:124, 0:124]).then_inc(tp_ready, 1)
                        pe.wait_ge(masked, 1)
                        blocks(H_INIT, lambda b: tile[6][:, P * b:P * (b + 1)], 4)
                        free(H_INIT + 1)
                        for k in range(2):
                            for t in range(T):
                                last = pe.transpose(half_tile(H_INIT + 1)[:, k, P * t:P * (t + 1)],
                                                    tok(5)[:, 0, 256 * t + P * k:256 * t + P * (k + 1)], ident[:])
                        last.then_inc(tp_ready, 1)
                        pe.matmul(sp[0][0:32, 0:384], tile[4][0:33, 896:928], tile[4][0:33, 0:384],
                                  start=True, stop=True).then_inc(bias_psum, 1)
                    if (u, c) == (2, 4):
                        wait_left(pe, U_A)
                        to_features(H_HC, tok(3))
                    if (u, c) == (4, 4):
                        wait_left(pe, U_CG)
                        to_features(H_SC, tok(3))
                    if (u, c) == (5, 4):
                        wait_left(pe, U_BG)
                        to_features(H_BG, tok(2))
                    if (u, c) == (6, 4):
                        wait_left(pe, U_D)
                        to_features(H_PZ, tok(3))
                    if (u, c) == (7, 2):
                        pe.wait_ge(pooled, 1)
                        for f in range(4):
                            if f % 2 == 0:
                                free(H_PO + f // 2)
                            last = pe.matmul(half_tile(H_PO + f // 2)[:, f % 2], tile[7][:, 512 + P * f:512 + P * (f + 1)],
                                             feat(5 + f % 2)[:, f], start=True, stop=True)
                            if f % 2:
                                last.then_inc(tp_ready, 1)
            wait_half_left(pe, H_INIT + 1)
            for j in range(4):
                chunk(START[PROJ_UNIT + j], PROJ_UNIT + j, 0, hh[:, 12:14], hl[:, 12:14])
                if j == 1:
                    pe.wait_ge(conv, 3 * TAPS)
                    pe.wait_ge(conv_pool, TAPS)
                    blocks(H_CB, lambda b: feat(1)[:, b % 4, P * (b // 4):P * (b // 4 + 1)])
                if j == 2:
                    pe.wait_ge(sgu_ready, 1)
                    pe.wait_ge(bias_sb, 1)
                    for t in range(T):
                        for h in range(4):
                            last = pe.matmul(sp[t][:, P * h:P * (h + 1)], tile[7][:, P * h:P * (h + 1)],
                                             tok(2)[:, t, P * h:P * (h + 1)], start=True, stop=True)
                    last.then_inc(sgu_sum, 1)
                if j == 3:
                    wait_half_left(pe, H_CB + 1)
                    to_features(H_CN, tok(4))
            for j in range(NG):
                for c in range(8):
                    u = OUT_UNIT + j
                    if j == 0 and c == 0:
                        pe.wait_ge(mix_ready, 1)
                        wait_half_left(pe, H_PO + 1)
                    if j == 0 and c == 4:
                        wait_half_left(pe, H_OA + 1)
                    if j == 0 and c == 6:
                        pe.wait_ge(mix_ready, 2)
                    chunk(START[u] + c, u, c, hh, hl)
                    if (j, c) == (0, 1):
                        pe.wait_ge(oa_ready, 1)
                        to_features(H_OA, tok(5))
                    if j and c == 2:
                        wait_left(pe, u - 1)
                        to_features(H_FFN + 2 * (j - 1), resid[:, :, CW * (j - 1):CW * j])

            def pair(s, u, lap, half=None, first=False):
                for c in range(16):
                    if first and c == 6:
                        wait_half_left(pe, H_FFN + 7)
                    chunk(s + c, u + c // 8, c % 8, yh, yl, lap)
                    if first and c == 2:
                        wait_left(pe, OUT_UNIT + 3)
                        to_features(H_FFN + 6, resid[:, :, 3 * CW:])
                    if half is not None and c == 2:
                        wait_left(pe, u - 1, lap)
                        to_features(half, tok(1), lap)

            wait_half_left(pe, H_FFN + 5)
            pair(START[FFN_UNIT], FFN_UNIT, ONCE, first=True)
            with pe.Fori(0, 2) as r:
                with pe.Fori(0, 3) as j:
                    pair(START[FFN_UNIT + 2], FFN_UNIT + 2, Lap.at(r, j), H_HID)
                lap = Lap.at(r)
                for d in range(4):
                    for c in range(8):
                        if (d, c) == (0, 0):
                            wait_half_left(pe, H_HID + 5, lap)
                        if (d, c) == (0, 6):
                            wait_half_left(pe, H_HID + 7, lap)
                        chunk(START[FFN_UNIT + 8 + d] + c, FFN_UNIT + 8 + d, c, hh, hl, lap)
                        if (d, c) == (0, 2):
                            wait_left(pe, FFN_UNIT + 7, lap)
                            to_features(H_HID + 6, tok(1), lap)
                pair(START[FFN_UNIT + 12], FFN_UNIT + 12, lap)
            base = FFN_UNIT + 26
            with pe.Fori(0, 2) as j:
                pair(START[base], base, Lap(2 * j, j, j, 2 * j), H_HID + 16)
            for d in range(4):
                for c in range(6):
                    u = base + 4 + d
                    if (d, c) == (0, 0):
                        wait_half_left(pe, H_HID + 19)
                    if (d, c) == (0, 4):
                        wait_half_left(pe, H_HID + 21)
                    chunk(START[u] + c, u, c, hh, hl)
                    if (d, c) == (0, 2):
                        wait_left(pe, base + 3)
                        to_features(H_HID + 20, tok(1))
                    if d and c == 2:
                        wait_left(pe, u - 1)
                        to_features(H_PLE + 2 * (d - 1), resid[:, :, CW * (d - 1):CW * d])

            for j in range(NG):
                for c in range(8):
                    u = PLE_UNIT + j
                    if (j, c) == (0, 0):
                        wait_half_left(pe, H_PLE + 5)
                    if (j, c) == (0, 6):
                        wait_half_left(pe, H_PLE + 7)
                    chunk(START[u] + c, u, c, yh, yl)
                    if j == 0 and c == 2:
                        wait_left(pe, u - 1)
                        to_features(H_PLE + 6, resid[:, :, 3 * CW:])
                    if j and c == 2:
                        pe.wait_ge(x1_ready, j)
                        to_features(H_SWA + 2 * (j - 1), resid[:, :, CW * (j - 1):CW * j])

            def score(g, r):
                n = 3 * g + r
                t, h0, nh, nk = ROUNDS[r]
                if n:
                    pe.wait_ge(scored, n)
                if r == 0:
                    wait_half_left(pe, H_Q[g] + 1)
                w = P * nk
                for i in range(nh):
                    h = h0 + i
                    rows_ = slice(HD * (h % 2), HD * (h % 2) + HD)
                    last = pe.matmul(sp[i % 2][:, w * (i // 2):w * (i // 2) + w],
                                     feat(4)[rows_, h // 2, P * t:P * (t + 1)], feat(3)[rows_, g, 2 * P - w:2 * P],
                                     start=True, stop=True)
                last.then_inc(scores, 1)

            def turn(g, r):
                n = 3 * g + r
                pe.wait_ge(expd, n + 1)
                blocks(H_PT[g, r], lambda b: tile[(2, 6)[n % 2]][:, P * b:P * (b + 1)])

            def weigh(g, r):
                t, h0, nh, nk = ROUNDS[r]
                wait_half_left(pe, H_PT[g, r] + 1)
                h = H_PV[g, r]
                free(h)
                for i in range(nh):
                    for k in range(nk):
                        last = pe.matmul(tp[h % 2][:, HD * i:HD * (i + 1)], tile[7][:, P * (nk * i + k):P * (nk * i + k + 1)],
                                         tok(0)[:, T - nk + k, 256 + HD * g:256 + HD * (g + 1)], start=(k == 0), stop=(k == nk - 1))
                last.then_inc(tp_ready, 1)

            for v in range(9):
                for c in range(8):
                    u = SWA_UNIT + v
                    if (v, c) == (0, 0):
                        wait_half_left(pe, H_SWA + 5)
                    if (v, c) == (0, 6):
                        wait_half_left(pe, H_SWA + 7)
                    chunk(START[u] + c, u, c, hh, hl)
                    if (v, c) == (0, 2):
                        pe.wait_ge(x1_ready, 4)
                        to_features(H_SWA + 6, resid[:, :, 3 * CW:])
                    if (v, c) == (1, 4):
                        wait_left(pe, SWA_UNIT)
                        for t in range(T):
                            last = pe.matmul(sp[t][:], flip[:], tok(0)[:, T - 1 - t], start=True, stop=True)
                        last.then_inc(kv_flipped, 1)
                    if (v, c) == (2, 3):
                        pe.wait_ge(kd_ready, 1)
                        to_features(H_K, tok(2))
                    if c == 0 and 3 <= v <= 6:
                        score(v - 3, 1)
                    if c == 1 and 4 <= v <= 7:
                        weigh(v - 4, 2)
                    if c == 2 and 3 <= v <= 6:
                        turn(v - 3, 0)
                        score(v - 3, 2)
                    if c == 3 and 3 <= v <= 6:
                        weigh(v - 3, 0)
                    if c == 4 and 3 <= v <= 6:
                        turn(v - 3, 1)
                    if c == 5 and 2 <= v <= 5:
                        wait_left(pe, u - 1)
                        to_features(H_Q[v - 2], tok(1))
                    if c == 5 and v >= 6:
                        pe.wait_ge(og_ready, v - 5)
                        g = v - 6
                        to_features(H_OG[g], wide[:, :, CW * g:CW * (g + 1)])
                    if c == 6 and 2 <= v <= 5:
                        score(v - 2, 0)
                    if c == 6 and 3 <= v <= 6:
                        weigh(v - 3, 1)
                    if c == 7 and 3 <= v <= 6:
                        turn(v - 3, 2)
            for j in range(NG):
                for c in range(8):
                    u = SO_UNIT + j
                    if (j, c) == (0, 0):
                        wait_half_left(pe, H_OG[1] + 1)
                    if (j, c) == (0, 4):
                        wait_half_left(pe, H_OG[2] + 1)
                    if (j, c) == (0, 6):
                        wait_half_left(pe, H_OG[3] + 1)
                    chunk(START[u] + c, u, c, yh, yl)
                    if (j, c) == (0, 3):
                        pe.wait_ge(og_ready, 4)
                        to_features(H_OG[3], wide[:, :, 3 * CW:])


_INS = ["x", "p", "norm_mix_g", "w_in", "sgu_ln_g", "sgu_ln_b", "sgu_w", "sgu_b", "sc_conv_w", "cf_conv_w",
        "cf_conv_b", "cf_ln_g", "cf_ln_b", "pool_w", "pool_scale", "w_out", "norm_ffn_g", "w_gate", "w_up",
        "w_down", "norm_ple_g", "w_ple_gate", "w_ple_proj", "final_norm_g", "rel_bias_2", "swa_norm_2",
        "swa_w_in_2", "swa_q_gain_2", "swa_k_gain_2", "swa_sinks_2", "swa_w_out_2"]


def kernel(**inputs):
    import numpy as _np
    import concourse.bacc as _bacc
    from concourse import mybir as _mybir
    from concourse.bass_utils import run_bass_kernel_spmd as _run

    nc = _bacc.Bacc("TRN2", target_bir_lowering=False, num_devices=1)
    arrays, args = {}, []
    for name in _INS:
        a = _np.ascontiguousarray(inputs[name])
        arrays[f"in_{name}"] = a
        args.append(nc.dram_tensor(f"in_{name}", a.shape, _mybir.dt.from_np(a.dtype), kind="ExternalInput").ap())
    for name, a in (("buckets", bucket_rows()), ("counts", pool_counts())):
        arrays[f"const_{name}"] = a
        args.append(nc.dram_tensor(f"const_{name}", a.shape, _mybir.dt.float32, kind="ExternalInput").ap())
    out = nc.dram_tensor("out", (1, S, D), _mybir.dt.float32, kind="ExternalOutput").ap()
    bias_rows = nc.dram_tensor("bias_rows", (32, 3 * P), _mybir.dt.float32, kind="Internal").ap()
    build(nc, *args, out, bias_rows)
    r = _run(nc, [arrays], core_ids=[0])
    return r.results[0]["out"]
```
